# Optimizing a Trainium2 kernel written in Bass

```python
import jax, jax.numpy as jnp
from jax import lax
import numpy as np

D_MODEL = 1024
BATCH = 1
SEQ = 256
DEPTH = 1

CHUNK = 64
N_LEFT_CHUNKS = 8
BAND = (N_LEFT_CHUNKS + 1) * CHUNK
ATT_HEADS = 8
HEAD_DIM = 64
ATT_WIDTH = ATT_HEADS * HEAD_DIM
MAX_REL = 128
SGU_BLOCK = 128
SGU_GROUPS = 8
SGU_WIDTH = 512
SGU_GROUP_DIM = SGU_WIDTH // SGU_GROUPS
IN_WIDTH = 3 * ATT_WIDTH + 2 * SGU_WIDTH
N_BRANCHES = 2
N_EXPERTS = 32
TOP_K = 4
D_EXPERT = D_MODEL
SWIGLU_LIMIT = 7.0
SWIGLU_ALPHA = 1.702
EXPERT_BLOCK = 256
N_MOD = 6
EPS = 1e-6

kernel_name = "hybrid_chunk_attn_gmlp_moe_block"

def rmsnorm(x, g):
    xf = x.astype(jnp.float32)
    y = xf * lax.rsqrt(jnp.mean(xf * xf, axis=-1, keepdims=True) + EPS)
    return (y * g.astype(jnp.float32)).astype(x.dtype)

def layernorm(x, g, b):
    xf = x.astype(jnp.float32)
    mu = jnp.mean(xf, axis=-1, keepdims=True)
    var = jnp.mean(jnp.square(xf - mu), axis=-1, keepdims=True)
    y = (xf - mu) * lax.rsqrt(var + EPS)
    return (y * g.astype(jnp.float32) + b.astype(jnp.float32)).astype(x.dtype)

def chunk_attention(q, k, v, rel_bias):
    B, S, _ = q.shape
    n_chunks = S // CHUNK
    q = q.reshape(B, n_chunks, CHUNK, ATT_HEADS, HEAD_DIM)
    k = k.reshape(B, n_chunks, CHUNK, ATT_HEADS, HEAD_DIM)
    v = v.reshape(B, n_chunks, CHUNK, ATT_HEADS, HEAD_DIM)
    pad = ((0, 0), (N_LEFT_CHUNKS, 0), (0, 0), (0, 0), (0, 0))
    kp = jnp.pad(k, pad)
    vp = jnp.pad(v, pad)
    kb = jnp.concatenate([kp[:, j:j + n_chunks] for j in range(N_LEFT_CHUNKS + 1)], axis=2)
    vb = jnp.concatenate([vp[:, j:j + n_chunks] for j in range(N_LEFT_CHUNKS + 1)], axis=2)
    scores = jnp.einsum('bcqhd,bckhd->bchqk', q, kb).astype(jnp.float32) * (HEAD_DIM ** -0.5)
    rel = (N_LEFT_CHUNKS * CHUNK + jnp.arange(CHUNK, dtype=jnp.int32)[:, None]) \
        - jnp.arange(BAND, dtype=jnp.int32)[None, :]
    idx = jnp.clip(rel, -MAX_REL, MAX_REL) + MAX_REL
    bias = rel_bias[:, idx].astype(jnp.float32)
    scores = scores + bias[None, None]
    kpos = jnp.arange(n_chunks, dtype=jnp.int32)[:, None] * CHUNK - N_LEFT_CHUNKS * CHUNK \
        + jnp.arange(BAND, dtype=jnp.int32)[None, :]
    valid = (kpos >= 0)[None, :, None, None, :]
    scores = jnp.where(valid, scores, -1e30)
    p = jax.nn.softmax(scores, axis=-1).astype(v.dtype)
    o = jnp.einsum('bchqk,bckhd->bcqhd', p, vb)
    return o.reshape(B, S, ATT_WIDTH)

def spatial_gating(z, ln_g, ln_b, w_s, b_s):
    B, S, _ = z.shape
    z = jax.nn.gelu(z, approximate=False)
    u, vv = jnp.split(z, 2, axis=-1)
    vv = layernorm(vv, ln_g, ln_b)
    n_blocks = S // SGU_BLOCK
    vv = vv.reshape(B, n_blocks, SGU_BLOCK, SGU_GROUPS, SGU_GROUP_DIM)
    causal = jnp.tril(jnp.ones((SGU_BLOCK, SGU_BLOCK), dtype=w_s.dtype))
    wm = w_s * causal[None]
    s = jnp.einsum('gts,bnsgd->bntgd', wm, vv) + b_s.T[None, None, :, :, None]
    return u * s.reshape(B, S, SGU_WIDTH)

def moe_ffn(h, w_router, b_router, w_gate_up, b_gate_up, w_down, b_down):
    B, S, D = h.shape
    xt = h.reshape(-1, D)
    N = xt.shape[0]
    logits = (xt @ w_router + b_router).astype(jnp.float32)
    top_v, top_i = lax.top_k(logits, TOP_K)
    gates = jax.nn.softmax(top_v, axis=-1).astype(h.dtype)
    n_assign = N * TOP_K
    flat_e = top_i.reshape(-1).astype(jnp.int32)
    flat_tok = jnp.arange(n_assign, dtype=jnp.int32) // TOP_K
    flat_g = gates.reshape(-1)
    order = jnp.argsort(flat_e)
    sorted_e = flat_e[order]
    sorted_tok = flat_tok[order]
    sorted_g = flat_g[order]
    counts = jnp.zeros((N_EXPERTS,), jnp.int32).at[flat_e].add(1)
    padded = (counts + EXPERT_BLOCK - 1) // EXPERT_BLOCK * EXPERT_BLOCK
    pad_end = jnp.cumsum(padded)
    pad_start = pad_end - padded
    start = jnp.cumsum(counts) - counts
    rank = jnp.arange(n_assign, dtype=jnp.int32) - start[sorted_e]
    dest = pad_start[sorted_e] + rank
    n_blocks = -(-n_assign // EXPERT_BLOCK) + N_EXPERTS
    P = n_blocks * EXPERT_BLOCK
    buf_tok = jnp.zeros((P,), jnp.int32).at[dest].set(sorted_tok)
    buf_g = jnp.zeros((P,), h.dtype).at[dest].set(sorted_g)
    block_start = jnp.arange(n_blocks, dtype=jnp.int32) * EXPERT_BLOCK
    block_e = jnp.minimum(jnp.searchsorted(pad_end, block_start, side='right'), N_EXPERTS - 1)
    xb = xt[buf_tok].reshape(n_blocks, EXPERT_BLOCK, D)

    def expert_block(args):
        xblk, e = args
        gu = xblk @ w_gate_up[e] + b_gate_up[e]
        x_glu = jnp.minimum(gu[:, :D_EXPERT], SWIGLU_LIMIT)
        x_lin = jnp.clip(gu[:, D_EXPERT:], -SWIGLU_LIMIT, SWIGLU_LIMIT)
        act = x_glu * jax.nn.sigmoid(SWIGLU_ALPHA * x_glu) * (x_lin + 1)
        return act @ w_down[e] + b_down[e]

    yb = lax.map(expert_block, (xb, block_e)).reshape(P, D)
    out = jnp.zeros_like(xt).at[buf_tok].add(yb * buf_g[:, None])
    return out.reshape(B, S, D)

def setup_inputs(seed: int = 0) -> dict:
    key = jax.random.key(seed)
    ks = jax.random.split(key, 26)
    L, D = DEPTH, D_MODEL

    def nrm(k, shape, scale):
        return jax.random.normal(k, shape, jnp.float32) * scale

    return {
        "x": nrm(ks[0], (BATCH, SEQ, D), 1.0),
        "c": nrm(ks[1], (BATCH, D), 1.0),
        "w_ada": nrm(ks[2], (L, D, N_MOD * D), D ** -0.5),
        "b_ada": nrm(ks[3], (L, N_MOD * D), 0.02),
        "g_pre_mix": 1.0 + nrm(ks[4], (L, D), 0.05),
        "g_post_mix": 1.0 + nrm(ks[5], (L, D), 0.05),
        "w_in": nrm(ks[6], (L, D, IN_WIDTH), D ** -0.5),
        "rel_bias": nrm(ks[7], (L, ATT_HEADS, 2 * MAX_REL + 1), 0.5),
        "sgu_ln_g": 1.0 + nrm(ks[8], (L, SGU_WIDTH), 0.05),
        "sgu_ln_b": nrm(ks[9], (L, SGU_WIDTH), 0.02),
        "w_spatial": nrm(ks[10], (L, SGU_GROUPS, SGU_BLOCK, SGU_BLOCK), 0.5 * SGU_BLOCK ** -0.5),
        "b_spatial": 1.0 + nrm(ks[11], (L, SGU_GROUPS, SGU_BLOCK), 0.1),
        "w_branch_a": nrm(ks[12], (L, ATT_WIDTH, D), ATT_WIDTH ** -0.5),
        "w_branch_b": nrm(ks[13], (L, SGU_WIDTH, D), SGU_WIDTH ** -0.5),
        "w_gate": nrm(ks[14], (L, D, N_BRANCHES * D), D ** -0.5),
        "b_gate": nrm(ks[15], (L, N_BRANCHES * D), 0.02),
        "w_out": nrm(ks[16], (L, D, D), D ** -0.5),
        "g_pre_ffn": 1.0 + nrm(ks[17], (L, D), 0.05),
        "g_post_ffn": 1.0 + nrm(ks[18], (L, D), 0.05),
        "w_router": nrm(ks[19], (L, D, N_EXPERTS), D ** -0.5),
        "b_router": nrm(ks[20], (L, N_EXPERTS), 0.01),
        "w_gate_up": nrm(ks[21], (L, N_EXPERTS, D, 2 * D_EXPERT), D ** -0.5),
        "b_gate_up": nrm(ks[22], (L, N_EXPERTS, 2 * D_EXPERT), 0.02),
        "w_down": nrm(ks[23], (L, N_EXPERTS, D_EXPERT, D), D_EXPERT ** -0.5),
        "b_down": nrm(ks[24], (L, N_EXPERTS, D), 0.02),
    }

def reference(x, c, w_ada, b_ada, g_pre_mix, g_post_mix, w_in, rel_bias, sgu_ln_g, sgu_ln_b,
              w_spatial, b_spatial, w_branch_a, w_branch_b, w_gate, b_gate, w_out,
              g_pre_ffn, g_post_ffn, w_router, b_router, w_gate_up, b_gate_up, w_down, b_down):
    c_act = jax.nn.silu(c)
    for l in range(DEPTH):
        mod = (c_act @ w_ada[l] + b_ada[l])[:, None, :]
        sh1, sc1, gt1, sh2, sc2, gt2 = jnp.split(mod, N_MOD, axis=-1)

        h = rmsnorm(x, g_pre_mix[l]) * (1 + sc1) + sh1
        proj = h @ w_in[l]
        q = proj[..., :ATT_WIDTH]
        k = proj[..., ATT_WIDTH:2 * ATT_WIDTH]
        v = proj[..., 2 * ATT_WIDTH:3 * ATT_WIDTH]
        z = proj[..., 3 * ATT_WIDTH:]
        y_a = chunk_attention(q, k, v, rel_bias[l])
        y_b = spatial_gating(z, sgu_ln_g[l], sgu_ln_b[l], w_spatial[l], b_spatial[l])
        gates = jax.nn.sigmoid(h @ w_gate[l] + b_gate[l])
        g_a, g_b = jnp.split(gates, N_BRANCHES, axis=-1)
        merged = g_a * (y_a @ w_branch_a[l]) + g_b * (y_b @ w_branch_b[l])
        y = rmsnorm(merged @ w_out[l], g_post_mix[l])
        x = x + gt1 * y

        h = rmsnorm(x, g_pre_ffn[l]) * (1 + sc2) + sh2
        y = moe_ffn(h, w_router[l], b_router[l], w_gate_up[l], b_gate_up[l], w_down[l], b_down[l])
        y = rmsnorm(y, g_post_ffn[l])
        x = x + gt2 * y
    return x


_drawn_inputs = setup_inputs


def setup_inputs(seed=0):
    import zlib

    import numpy as np

    out = dict(_drawn_inputs(seed))
    spreads = {}
    factors = {'b_gate': 4.127, 'b_gate_up': 6.096, 'b_down': 8.0, 'sgu_ln_g': 3.2, 'sgu_ln_b': 3.494}
    for name, (base, spread) in spreads.items():
        noise = np.random.default_rng([zlib.crc32(name.encode()), seed]).standard_normal(out[name].shape)
        drawn = base * np.exp(spread * noise) if base else spread * noise
        out[name] = __import__('jax').numpy.asarray(drawn.astype(out[name].dtype))
    for name, factor in factors.items():
        out[name] = (out[name] * factor).astype(out[name].dtype)
    return out
```

```python
from contextlib import ExitStack

import concourse.bass as bass
from concourse import mybir

ALU = mybir.AluOpType
ACT = mybir.ActivationFunctionType
F32 = mybir.dt.float32
I32 = mybir.dt.int32
AX = mybir.AxisListType

P = 128
TOK, D = 256, 1024
TT = TOK // P
KD = D // P
AW = 512
KA = AW // P
HEADS, HD = 8, 64
NREL = 257
GROUPS = 8
NMOD = 6
NEXP, TOPK = 32, 4
F = 1024
TB = 32
CT = P // TB
QF = F // CT
NBLK = TOK // TB
LIMIT, ALPHA, EPS = 7.0, 1.702, 1e-6
NEG = -1e30
BW = 3 * P
PAGE = 4096
RING = 5

PAGES = [("dve", "ada", 0, 0), ("dve", "ada", 0, 1), ("dve", "ada", 1, 0), ("dve", "ada", 1, 1)]
for _n, _name in enumerate(("q", "k", "v", "vv")):
    PAGES += [("pe", _name, 0, 0), ("dve", "ada", _n + 2, 0), ("dve", "ada", _n + 2, 1)]
PAGES += [("pe", "u", 0, 0)] + [("pe", "gate", _n, 0) for _n in range(4)]
PAGES += [("pe", "ba", 0, 0), ("pe", "bb", 0, 0), ("pe", "wo", 0, 0), ("pe", "wo", 1, 0)]
IN_COL = {"q": 0, "k": AW, "v": 2 * AW, "u": 3 * AW, "vv": 4 * AW}


def page_of(name, part=0, half=0):
    return [n for n, pg in enumerate(PAGES) if pg[1:] == (name, part, half)][0]


def consumed(n):
    who, name, i, _ = PAGES[n]
    if who == "dve":
        return "dve_page", sum(1 for pg in PAGES[:n + 1] if pg[0] == "dve")
    if name in ("ba", "bb"):
        return "branch", KD
    if name == "wo":
        return "wo", TT
    return "proj", 4 + 2 * sum(1 for pg in PAGES[:n + 1] if pg[0] == "pe")


def block_program(nc, x, c, w_ada, b_ada, g_pre_mix, g_post_mix, w_in, rel_rev, sgu_ln_g, sgu_ln_b,
                  w_spatial, b_spatial, w_branch_a, w_branch_b, w_gate, b_gate, w_out, g_pre_ffn,
                  g_post_ffn, w_router, b_router, w_gate_up, b_gate_up, w_down, b_down, out):
    with ExitStack() as ctx:
        def sb(name, shape, dt=F32):
            return ctx.enter_context(nc.sbuf_tensor(name, shape, dt))

        def psum(name, shape):
            return ctx.enter_context(nc.psum_tensor(name, shape, F32))

        def sem(name):
            return ctx.enter_context(nc.semaphore(name))

        arena = sb("arena", [P, 11 * PAGE])

        def page(n, cols=PAGE):
            return arena[:, n * PAGE:n * PAGE + cols]

        def part(start, cols):
            return arena[:, start:start + cols]

        at5 = 5 * PAGE
        acc = part(at5, 2 * D).rearrange("p (b d) -> p b d", b=2)
        qT = part(at5 + 2048, KA * TOK).rearrange("p (m t) -> p m t", m=KA)
        kT = part(at5 + 3072, KA * TOK).rearrange("p (m t) -> p m t", m=KA)
        v_sb = part(at5 + 4096, TT * AW).rearrange("p (t w) -> p t w", t=TT)
        vv = part(at5 + 5120, TT * AW).rearrange("p (t w) -> p t w", t=TT)
        bias = part(at5 + 6144, HEADS * TOK).rearrange("p (h k) -> p h k", h=HEADS)
        wsT = part(at5 + 8192, GROUPS * P).rearrange("p (g t) -> p g t", g=GROUPS)
        ws = part(at5 + 9216, GROUPS * P).rearrange("p (g s) -> p g s", g=GROUPS)
        bsb = part(at5 + 10240, KA * P).rearrange("p (m t) -> p m t", m=KA)
        ybT = part(at5 + 10752, KA * TOK).rearrange("p (m t) -> p m t", m=KA)
        at8 = 8 * PAGE
        x_sb = part(at8, TT * D).rearrange("p (t d) -> p t d", t=TT)
        hT = part(at8 + 2048, KD * TOK).rearrange("p (k t) -> p k t", k=KD)
        mergedT = hT
        gates = part(at8 + 4096, 2 * KD * TOK).rearrange("p (m t) -> p m t", m=2 * KD)
        h2T = part(at8 + 4096, KD * TOK).rearrange("p (k t) -> p k t", k=KD)
        shift = part(at8 + 8192, D)
        scale = part(at8 + 9216, D)
        gain1 = part(at8 + 10240, D)
        yaT = part(at8 + 11264, KA * TOK).rearrange("p (m t) -> p m t", m=KA)

        gu_w = [part(b * 4 * PAGE, 4 * PAGE).rearrange("p (k s f) -> p k s f", k=KD, s=2) for b in range(2)]
        dlo_w = [page(8 + b).rearrange("p (k d) -> p k d", k=4) for b in range(2)]
        dhi_w = page(10).rearrange("p (k d) -> p k d", k=4)
        x1_back = page(0, TT * D).rearrange("p (t d) -> p t d", t=TT)
        y_out = page(1, TT * D).rearrange("p (t d) -> p t d", t=TT)

        h_sb = sb("h_sb", [P, TT, D])
        gain2 = sb("gain2", [P, D])
        ident = sb("ident", [P, P])
        ones = sb("ones", [P, P])
        before = sb("before", [P, P])
        iota = sb("iota", [P, CT, TB])
        rank_tab = sb("rank_tab", [P, TT, NBLK, NEXP])
        gate_tab = sb("gate_tab", [P, TT, NEXP])
        nblk_i = sb("nblk_i", [P, NEXP], I32)
        bgu = sb("bgu", [8, 2, QF])
        pick8 = sb("pick8", [8, 8, TB])
        work = sb("work", [P, 2624])
        prob = work[:, 0:2 * BW].rearrange("p (b k) -> p b k", b=2)
        probT = work[:, 768:768 + BW]
        ln_g = work[:, 1152:1152 + AW]
        ln_b = work[:, 1664:1664 + AW]
        wr = work[:, 2176:2176 + KD * NEXP].rearrange("p (k e) -> p k e", k=KD)
        sel = work[:, 0:64].rearrange("p (t j) -> p t j", t=TT)
        selg = work[:, 64:320].rearrange("p (t c j) -> p t c j", t=TT, c=CT)
        selgT = work[:, 320:576].rearrange("p (t n) -> p t n", t=TT)
        hgT = work[:, 576:832].rearrange("p (k j) -> p k j", k=KD)
        glu = work[:, 832:1088]
        sig = work[:, 1088:1344]
        lin = work[:, 1344:1600]
        tmp = work[:, 1600:1856]
        act_sb = work[:, 1856:2112].rearrange("p (h f) -> p h f", h=2)
        actT = work[:, 2112:2368].rearrange("p (h n) -> p h n", h=2)
        y_sb = work[:, 2368:2624]
        small = sb("small", [P, 448])
        c_act = small[:, 0:8]
        c_sig = small[:, 8:16]
        c_col = small[:, 16:24]
        ssq = small[:, 24:32]
        rms = small[:, 32:40]
        rstd = small[:, 40:48]
        bg_col = small[:, 48:64]
        stats = small[:, 64:76].rearrange("p (t s) -> p t s", t=TT)
        meanvar = small[:, 76:80].rearrange("p (t s) -> p t s", t=TT)
        nmax = small[:, 80:84].rearrange("p (b s) -> p b s", b=2)
        psm = small[:, 84:88].rearrange("p (b s) -> p b s", b=2)
        prc = small[:, 88:92].rearrange("p (b s) -> p b s", b=2)
        b_rt = small[:, 96:128]
        logit = small[:, 128:192].rearrange("p (t e) -> p t e", t=TT)
        top8 = small[:, 192:208].rearrange("p (t e) -> p t e", t=TT)
        above = small[:, 208:272].rearrange("p (t e) -> p t e", t=TT)
        equal = small[:, 272:336].rearrange("p (t e) -> p t e", t=TT)
        upto = small[:, 336:400].rearrange("p (t e) -> p t e", t=TT)
        r1 = small[:, 400:408]
        thr = small[:, 408:415]
        eps_col = small[:, 416:417]
        rt = work[:, 0:768]
        chosen = rt[:, 0:64].rearrange("p (t e) -> p t e", t=TT)
        expo = rt[:, 64:128].rearrange("p (t e) -> p t e", t=TT)
        rank = rt[:, 128:192].rearrange("p (t e) -> p t e", t=TT)
        cmp7 = rt[:, 192:192 + 7 * NEXP].rearrange("p (e m) -> p e m", m=7)
        nblk_f = rt[:, 448:480]
        gateT = rt[0:NEXP, 512:768].rearrange("p (t n) -> p t n", t=TT)
        c8 = h_sb[0:8, 0, 0:P]
        brow = work[0:HEADS, 0:BW]
        bd_sb = part(at5, D)[0:NEXP, :]

        pp = psum("pp", [P, 4, 512])
        po = psum("po", [P, 4, 512])

        bias_rows = nc.dram_tensor("bias_rows", [HEADS, P, BW], F32)
        x1_dram = nc.dram_tensor("x1_dram", [P, TT, D], F32)

        s_page = [sem(f"s_page{i}") for i in range(RING)]
        s_dve_page = sem("s_dve_page")
        s_x, s_c, s_ws = sem("s_x"), sem("s_c"), sem("s_ws")
        s_ln, s_bs, s_bg, s_wr = sem("s_ln"), sem("s_bs"), sem("s_bg"), sem("s_wr")
        s_brow, s_bfill, s_brows, s_bias, s_bmask = (sem("s_brow"), sem("s_bfill"), sem("s_brows"),
                                                     sem("s_bias"), sem("s_bmask"))
        s_gain = [sem(f"s_gain{i}") for i in range(4)]
        s_acc0 = sem("s_acc0")
        s_accb = [sem(f"s_accb{i}") for i in range(2)]
        s_const, s_pool = sem("s_const"), sem("s_pool")
        s_cT, s_csig, s_cact = sem("s_cT"), sem("s_csig"), sem("s_cact")
        s_acc, s_adasum, s_mod_a, s_mod_v = sem("s_acc"), sem("s_adasum"), sem("s_mod_a"), sem("s_mod_v")
        s_wsp, s_wsT, s_wsm = sem("s_wsp"), sem("s_wsT"), sem("s_wsm")
        s_ssx, s_h0, s_h = sem("s_ssx"), sem("s_h0"), sem("s_h")
        s_proj, s_projev = sem("s_proj"), sem("s_projev")
        s_mv, s_lnsq, s_lnn, s_lng, s_lnd = sem("s_mv"), sem("s_lnsq"), sem("s_lnn"), sem("s_lng"), sem("s_lnd")
        s_sgu, s_yb = sem("s_sgu"), sem("s_yb")
        s_score, s_soft, s_exp, s_prob = sem("s_score"), sem("s_soft"), sem("s_exp"), sem("s_prob")
        s_pT, s_pTev, s_pv, s_ya = sem("s_pT"), sem("s_pTev"), sem("s_pv"), sem("s_ya")
        s_br, s_mg, s_merged = sem("s_br"), sem("s_mg"), sem("s_merged")
        s_wo, s_ssy, s_x1, s_ssx1, s_h2 = sem("s_wo"), sem("s_ssy"), sem("s_x1"), sem("s_ssx1"), sem("s_h2")
        s_spill, s_h2p, s_h2T, s_lg, s_ngm, s_ex = (sem("s_spill"), sem("s_h2p"), sem("s_h2T"), sem("s_lg"),
                                                    sem("s_ngm"), sem("s_ex"))
        s_chosen, s_rank, s_tabs, s_gT, s_gTev, s_bdl = (sem("s_chosen"), sem("s_rank"), sem("s_tabs"),
                                                               sem("s_gT"), sem("s_gTev"), sem("s_bdl"))
        s_dve = sem("s_dve")
        s_act = sem("s_act")
        s_gup = [[sem(f"s_gup{b}{i}") for i in range(4)] for b in range(2)]
        s_bgu = [sem(f"s_bgu{b}") for b in range(2)]
        s_dlo = [sem(f"s_dlo{b}") for b in range(2)]
        s_dhi = sem("s_dhi")
        s_sel, s_hg, s_hgT = sem("s_sel"), sem("s_hg"), sem("s_hgT")
        s_half, s_sgp = sem("s_half"), sem("s_sgp")
        s_gu, s_glu, s_lin, s_sig, s_tmp, s_actv = (sem("s_gu"), sem("s_glu"), sem("s_lin"), sem("s_sig"),
                                                    sem("s_tmp"), sem("s_actv"))
        s_aT, s_aTev, s_y, s_ysb = sem("s_aT"), sem("s_aTev"), sem("s_y"), sem("s_ysb")
        s_fin, s_ssf, s_x1b, s_yo, s_out = sem("s_fin"), sem("s_ssf"), sem("s_x1b"), sem("s_yo"), sem("s_out")

        ada_v = w_ada[0].rearrange("(k p) n -> p k n", p=P)
        in_v = w_in[0].rearrange("(k p) n -> p k n", p=P)
        gate_v = w_gate[0].rearrange("(k p) n -> p k n", p=P)
        ba_v = w_branch_a[0].rearrange("(k p) n -> p k n", p=P)
        bb_v = w_branch_b[0].rearrange("(k p) n -> p k n", p=P)
        wo_v = w_out[0].rearrange("(k p) n -> p k n", p=P)
        gu_v = w_gate_up[0].rearrange("e (k p) n -> e p k n", p=P)
        dn_v = w_down[0].rearrange("e (k p) n -> e p k n", p=P)
        bgu_v = b_gate_up[0].rearrange("e (r f) -> e r f", r=8)
        x_v = x[0].rearrange("(t p) d -> p t d", p=P)
        out_v = out[0].rearrange("(t p) d -> p t d", p=P)

        def page_src(n):
            _, name, i, half = PAGES[n]
            if name == "ada":
                return ada_v[:, 4 * half:4 * half + 4, i * D:(i + 1) * D]
            if name == "gate":
                return gate_v[:, :, i * 512:(i + 1) * 512]
            if name == "wo":
                return wo_v[:, 4 * i:4 * i + 4, :]
            if name in ("ba", "bb"):
                return {"ba": ba_v, "bb": bb_v}[name]
            return in_v[:, :, IN_COL[name]:IN_COL[name] + AW]

        def page_k(n, k):
            cols = D if PAGES[n][1] in ("ada", "wo", "ba", "bb") else AW
            return page(n % RING)[:, k * cols:(k + 1) * cols]

        def page_landed(eng, n):
            eng.wait_ge(s_page[n % RING], 16 * (n // RING + 1))

        def page_free(eng, n):
            signal, count = consumed(n)
            eng.wait_ge({"dve_page": s_dve_page, "branch": s_br, "wo": s_wo, "proj": s_proj}[signal], count)

        block = ctx.enter_context(nc.Block())

        @block.sync
        def _(sp):
            for n in range(len(PAGES)):
                if n >= RING:
                    page_free(sp, n - RING)
                src = page_src(n)
                sp.dma_start(page(n % RING).rearrange("p (k n) -> p k n", k=src.shape[1]),
                             src).then_inc(s_page[n % RING], 16)

            def load_gu(slot, e, i):
                sp.dma_start(gu_w[slot][:, 2 * i:2 * i + 2, :, :].rearrange("p k s f -> p k (s f)"),
                             gu_v[e, :, 2 * i:2 * i + 2, :]).then_inc(s_gup[slot][i], 16)

            def load_dlo(slot, e):
                sp.dma_start(dlo_w[slot], dn_v[e, :, 0:4, :]).then_inc(s_dlo[slot], 16)

            def load_dhi(e):
                sp.dma_start(dhi_w, dn_v[e, :, 4:8, :]).then_inc(s_dhi, 16)

            sp.dma_start(bgu[:, 0, :], bgu_v[0]).then_inc(s_bgu[0], 16)
            sp.dma_start(bgu[:, 1, :], bgu_v[1]).then_inc(s_bgu[1], 16)
            for i in range(4):
                page_free(sp, len(PAGES) - RING + i)
                load_gu(0, 0, i)
            page_free(sp, len(PAGES) - 1)
            load_gu(1, 1, 0)
            sp.wait_ge(s_br, KD)
            sp.wait_ge(s_sgp, 1)
            for i in range(1, 4):
                load_gu(1, 1, i)
            sp.wait_ge(s_spill, 16 * TT)
            sp.wait_ge(s_lg, TT)
            load_dlo(0, 0)
            load_dhi(0)
            load_dlo(1, 1)
            sp.wait_ge(s_tabs, 1)
            done = sp.alloc_register("sp_blocks")
            sp.reg_mov(done, 0)

            def count_blocks(e):
                nb = sp.value_load(nblk_i[0:1, bass.ds(e, 1)], min_val=1, max_val=NBLK)
                sp.reg_add(done, done, nb)
                return sp.snap(done, min_val=1, max_val=NEXP * NBLK)

            with sp.Fori(0, NEXP // 2 - 1) as i:
                for step in range(2):
                    slot = step
                    total = count_blocks(i * 2 + step)
                    sp.wait_ge(s_gu, total)
                    sp.dma_start(bgu[:, slot, :], bgu_v[i * 2 + (2 + step)]).then_inc(s_bgu[slot], 16)
                    for q in range(4):
                        load_gu(slot, i * 2 + (2 + step), q)
                    sp.wait_ge(s_y, total)
                    load_dhi(i * 2 + (1 + step))
                    load_dlo(slot, i * 2 + (2 + step))
            count_blocks(NEXP - 2)
            total = sp.snap(done, min_val=1, max_val=NEXP * NBLK)
            sp.wait_ge(s_gu, total)
            sp.wait_ge(s_y, total)
            load_dhi(NEXP - 1)
            sp.dma_start(x1_back, x1_dram[:, :, :]).then_inc(s_x1b, 16)
            for t in range(TT):
                sp.wait_ge(s_yo, t + 1)
                sp.dma_start(out_v[:, t, :], y_out[:, t, :]).then_inc(s_out, 16)
            sp.wait_ge(s_out, 16 * TT)

        @block.gpsimd
        def _(pool):
            g = nc.gpsimd
            g.memset(ident[:], 0.0).then_inc(s_pool, 1)
            g.memset(ones[:], 1.0).then_inc(s_pool, 1)
            g.memset(pick8[:], 0.0).then_inc(s_pool, 1)
            g.memset(acc[:, 0, :], 0.0).then_inc(s_acc0, 1)
            g.memset(acc[:, 1, :], 0.0).then_inc(s_acc0, 1)
            g.memset(eps_col, EPS).then_inc(s_pool, 1)
            pool.wait_ge(s_pool, 4)
            g.affine_select(out=ident[:], in_=ident[:], compare_op=ALU.not_equal, fill=1.0, base=0,
                            pattern=[[-1, P]], channel_multiplier=1).then_inc(s_const, 1)
            for n in range(2):
                pool.wait_ge(s_acc0, n + 1)
                pool.dma_start(acc[0:1, n, :], b_ada[:, n * D:(n + 1) * D]).then_inc(s_accb[n], 16)
            g.affine_select(out=before[:], in_=ones[:], compare_op=ALU.is_gt, fill=0.0, base=0,
                            pattern=[[1, P]], channel_multiplier=-1).then_inc(s_const, 1)
            g.affine_select(out=pick8[:], in_=pick8[:], compare_op=ALU.not_equal, fill=1.0, base=0,
                            pattern=[[-1, 8], [0, TB]], channel_multiplier=1).then_inc(s_const, 1)
            g.iota(iota[:], pattern=[[0, CT], [1, TB]], base=0, channel_multiplier=0,
                   allow_small_or_imprecise_dtypes=True).then_inc(s_const, 1)
            g.iota(thr, pattern=[[TB, 7]], base=TB, channel_multiplier=0,
                   allow_small_or_imprecise_dtypes=True).then_inc(s_const, 1)
            pool.wait_ge(s_bfill, 1)
            pool.dma_start(bias_rows[:, :, :],
                           brow.rearrange("h (a m) -> h a m", a=1).to_broadcast([HEADS, P, BW])).then_inc(s_brows, 16)
            pool.wait_ge(s_brows, 16)
            window = bass.AP(bias_rows, P - 1, [[BW - 1, P], [P * BW, HEADS], [1, TOK]])
            pool.dma_start(bias, window).then_inc(s_bias, 16)
            pool.wait_ge(s_bias, 16)
            g.memset(bias[0:HD, :, TOK - HD:TOK], NEG).then_inc(s_bmask, 1)
            pool.wait_ge(s_wsT, 2)
            g.affine_select(out=wsT, in_=wsT, compare_op=ALU.is_ge, fill=0.0, base=0,
                            pattern=[[0, GROUPS], [1, P]], channel_multiplier=-1).then_inc(s_wsm, 1)
            for t in range(TT):
                pool.wait_ge(s_h0, t + 1)
                pool.wait_ge(s_mod_a, 1)
                g.tensor_tensor(h_sb[:, t, :], h_sb[:, t, :], shift, ALU.add).then_inc(s_h, 1)
            for n in range(2, NMOD):
                pool.wait_ge(s_adasum, n - 1)
                g.memset(acc[:, n % 2, :], 0.0).then_inc(s_acc0, 1)
                pool.wait_ge(s_acc0, n + 1)
                pool.dma_start(acc[0:1, n % 2, :], b_ada[:, n * D:(n + 1) * D]).then_inc(s_accb[n % 2], 16)
                if n == 2:
                    pool.wait_ge(s_h, TT)
                    pool.wait_ge(s_h0, TT)
                    pool.dma_start(scale, g_pre_ffn[0:1, :].to_broadcast([P, D])).then_inc(s_gain[2], 16)
            for t in range(TT):
                pool.wait_ge(s_lnn, t + 1)
                pool.wait_ge(s_ln, 32)
                g.tensor_tensor(vv[:, t, :], vv[:, t, :], ln_g, ALU.mult).then_inc(s_lng, 1)
                pool.wait_ge(s_lng, t + 1)
                g.tensor_tensor(vv[:, t, :], vv[:, t, :], ln_b, ALU.add).then_inc(s_lnd, 1)
            pool.wait_ge(s_adasum, NMOD)
            pool.dma_start(bd_sb, b_down[0]).then_inc(s_bdl, 16)
            for m in range(KD):
                pool.wait_ge(s_mg, m + 1)
                g.tensor_tensor(mergedT[:, m, :], gates[:, m, :], gates[:, KD + m, :],
                                ALU.add).then_inc(s_merged, 1)
            for t in range(TT):
                pool.wait_ge(s_x1, t + 1)
                pool.dma_start(x1_dram[:, t, :], x_sb[:, t, :]).then_inc(s_spill, 16)
            pool.wait_ge(s_spill, 16 * TT)

        @block.scalar
        def _(act):
            a = nc.scalar
            act.dma_start(c8, c.rearrange("a (k p) -> (a k) p", p=P)).then_inc(s_c, 16)
            act.dma_start(x_sb, x_v).then_inc(s_x, 16)
            act.dma_start(ws, w_spatial[0].rearrange("g t s -> t g s")).then_inc(s_ws, 16)
            act.dma_start(brow[:, P - 1:BW], rel_rev[0]).then_inc(s_brow, 16)
            act.dma_start(scale, g_pre_mix[0:1, :].to_broadcast([P, D])).then_inc(s_gain[0], 16)
            act.dma_start(gain1, g_post_mix[0:1, :].to_broadcast([P, D])).then_inc(s_gain[1], 16)
            act.dma_start(gain2[:], g_post_ffn[0:1, :].to_broadcast([P, D])).then_inc(s_gain[3], 16)
            with nc.allow_non_contiguous_dma(reason="2048 biases, once"):
                act.dma_start(bg_col, b_gate[0].rearrange("(m p) -> p m", p=P)).then_inc(s_bg, 16)
            act.dma_start(ln_g, sgu_ln_g[0:1, :].to_broadcast([P, AW])).then_inc(s_ln, 16)
            act.dma_start(ln_b, sgu_ln_b[0:1, :].to_broadcast([P, AW])).then_inc(s_ln, 16)
            act.dma_start(wr, w_router[0].rearrange("(k p) e -> p k e", p=P)).then_inc(s_wr, 16)
            act.dma_start(b_rt, b_router[0:1, :].to_broadcast([P, NEXP])).then_inc(s_wr, 16)
            bs_v = b_spatial[0].rearrange("(m r) t -> r m t", r=2)
            for r in range(2):
                act.dma_start(bsb[HD * r:HD * r + HD, :, :],
                              bs_v[r:r + 1].to_broadcast([HD, KA, P])).then_inc(s_bs, 16)

            act.wait_ge(s_cact, 1)
            a.activation(c_sig, c_col, ACT.Sigmoid).then_inc(s_csig, 1)
            act.wait_ge(s_x, 16)
            act.wait_ge(s_cact, 2)
            for t in range(TT):
                a.activation(h_sb[:, t, :], x_sb[:, t, :], ACT.Square, accum_out=ssq[:, t:t + 1]).then_inc(s_act, 1)
            act.wait_ge(s_act, TT)
            act.wait_ge(s_pool, 4)
            a.activation(rms[:, 0:2], ssq[:, 0:2], ACT.Sqrt, scale=1.0 / D, bias=eps_col).then_inc(s_ssx, 1)
            for b in range(2):
                act.wait_ge(s_wsp, b + 1)
                a.copy(wsT[:, 4 * b:4 * b + 4, :].rearrange("p g t -> p (g t)"), po[:, b, :]).then_inc(s_wsT, 1)
            act.wait_ge(s_adasum, 1)
            a.copy(shift, po[:, 2:4, :].rearrange("p b n -> p (b n)")).then_inc(s_mod_a, 1)

            bank = 0

            def evac(dst, func, n_banks=1, **kw):
                nonlocal bank
                act.wait_ge(s_proj, bank + 1)
                a.activation(dst, pp[:, bank % 4, :], func, **kw).then_inc(s_projev, 1)
                bank += 1

            def heads(buf, b):
                return buf[:, 2 * b:2 * b + 2, :].rearrange("p m t -> p (m t)")

            for t in range(TT):
                for q in range(2):
                    act.wait_ge(s_proj, bank + 1)
                    a.activation(hT[:, 4 * q:4 * q + 4, t * P:(t + 1) * P],
                                 pp[:, bank % 4, :].rearrange("p (k t) -> p k t", k=4), ACT.Copy).then_inc(s_projev, 1)
                    bank += 1
            for b in range(2):
                evac(heads(qT, b), ACT.Copy, scale=float(HD) ** -0.5)
            for b in range(2):
                evac(heads(kT, b), ACT.Copy)
            act.wait_ge(s_adasum, 4)
            act.wait_ge(s_h, TT)
            a.copy(shift, po[:, 0:2, :].rearrange("p b n -> p (b n)")).then_inc(s_mod_a, 1)
            for t in range(TT):
                evac(v_sb[:, t, :], ACT.Copy)
            for t in range(TT):
                evac(vv[:, t, :], ACT.Gelu)
            for b in range(2):
                evac(heads(ybT, b), ACT.Gelu)
            act.wait_ge(s_mv, TT)
            a.activation(rms[:, 2:4], meanvar[:, :, 1], ACT.Sqrt, bias=eps_col).then_inc(s_lnsq, 1)

            def softmax_exp(h):
                act.wait_ge(s_soft, h + 1)
                a.activation(prob[:, h % 2, 0:P], prob[:, h % 2, 0:P], ACT.Exp, bias=nmax[:, h % 2, 0:1],
                             accum_out=psm[:, h % 2, 0:1])
                a.activation(prob[:, h % 2, P:BW], prob[:, h % 2, P:BW], ACT.Exp, bias=nmax[:, h % 2, 1:2],
                             accum_out=psm[:, h % 2, 1:2]).then_inc(s_exp, 1)

            softmax_exp(0)
            act.wait_ge(s_bg, 16)
            for h in range(HEADS):
                for i in range(2):
                    m = 2 * h + i
                    if i == 0:
                        act.wait_ge(s_proj, bank + 1)
                    ins = a.activation(gates[:, m, :], pp[:, bank % 4, i * TOK:(i + 1) * TOK], ACT.Sigmoid,
                                       bias=bg_col[:, m:m + 1])
                ins.then_inc(s_projev, 1)
                bank += 1
                act.wait_ge(s_pT, h + 1)
                a.activation(probT, po[:, 2, 0:BW], ACT.Copy).then_inc(s_pTev, 1)
                if h + 1 < HEADS:
                    softmax_exp(h + 1)

            for t in range(TT):
                act.wait_ge(s_wo, t + 1)
                a.activation(h_sb[:, t, :], po[:, 2 * t:2 * t + 2, :].rearrange("p b n -> p (b n)"), ACT.Square,
                             accum_out=ssq[:, 2 + t:3 + t]).then_inc(s_act, 1)
                act.wait_ge(s_act, TT + 2 * t + 1)
                a.activation(rms[:, 4 + t:5 + t], ssq[:, 2 + t:3 + t], ACT.Sqrt, scale=1.0 / D,
                             bias=eps_col).then_inc(s_ssy, 1)
                act.wait_ge(s_x1, t + 1)
                a.activation(h_sb[:, t, :], x_sb[:, t, :], ACT.Square, accum_out=ssq[:, 4 + t:5 + t]).then_inc(s_act, 1)
                act.wait_ge(s_act, TT + 2 * t + 2)
                a.activation(rms[:, 6 + t:7 + t], ssq[:, 4 + t:5 + t], ACT.Sqrt, scale=1.0 / D,
                             bias=eps_col).then_inc(s_ssx1, 1)
                for q in range(2):
                    act.wait_ge(s_h2p, 2 * t + q + 1)
                    ins = a.activation(h2T[:, 4 * q:4 * q + 4, t * P:(t + 1) * P],
                                       pp[:, q, :].rearrange("p (k t) -> p k t", k=4), ACT.Copy)
                    ins.then_inc(s_h2T, 1)
            act.wait_ge(s_ngm, 1)
            for t in range(TT):
                ins = a.activation(expo[:, t, :], logit[:, t, :], ACT.Exp, bias=r1[:, t:t + 1])
            ins.then_inc(s_ex, 1)
            act.wait_ge(s_gT, 1)
            a.activation(gateT.rearrange("p t n -> p (t n)"), pp[0:NEXP, 1, 0:TOK], ACT.Copy).then_inc(s_gTev, 1)

            item = act.alloc_register("act_item")
            act.reg_mov(item, 0)
            act.wait_ge(s_tabs, 1)
            act.wait_ge(s_ysb, 1)
            with act.Fori(0, NEXP) as e:
                nb = act.value_load(nblk_i[0:1, bass.ds(e, 1)], min_val=1, max_val=NBLK)
                with act.Fori(0, nb) as b:
                    act.reg_add(item, item, 1)
                    it = act.snap(item, min_val=1, max_val=NEXP * NBLK)
                    act.wait_ge(s_hg, it)
                    a.activation(hgT.rearrange("p k j -> p (k j)"), pp[:, 2, 0:TOK], ACT.Copy).then_inc(s_hgT, 1)
                    act.wait_ge(s_sgp, it + 1)
                    a.activation(selgT.rearrange("p t n -> p (t n)"), pp[:, 3, 256:512], ACT.Copy)
                    act.wait_ge(s_glu, it)
                    a.activation(sig, glu, ACT.Sigmoid, scale=ALPHA).then_inc(s_sig, 1)
                    act.wait_ge(s_aT, it)
                    a.activation(actT.rearrange("p h n -> p (h n)"), pp[:, 3, 0:256], ACT.Copy).then_inc(s_aTev, 1)
                    act.wait_ge(s_y, it)
                    a.activation(y_sb, pp[:, 1, 0:QF], ACT.Copy).then_inc(s_ysb, 1)

            for t in range(TT):
                act.wait_ge(s_fin, 1)
                a.activation(h_sb[:, t, :], po[:, 2 * t:2 * t + 2, :].rearrange("p b n -> p (b n)"), ACT.Square,
                             accum_out=ssq[:, t:t + 1]).then_inc(s_act, 1)
            act.wait_ge(s_act, 4 * TT)
            a.activation(rms[:, 0:2], ssq[:, 0:2], ACT.Sqrt, scale=1.0 / D, bias=eps_col).then_inc(s_ssf, 1)

        @block.vector
        def _(dve):
            v = nc.vector
            chain = 0

            def link(ins):
                nonlocal chain
                chain += 1
                ins.then_inc(s_dve, 1)
                dve.wait_ge(s_dve, chain)

            dve.wait_ge(s_cT, 1)
            v.tensor_copy(c_col, pp[:, 0, 0:KD]).then_inc(s_cact, 1)
            dve.wait_ge(s_cact, 1)
            dve.wait_ge(s_csig, 1)
            v.tensor_tensor(c_act, c_col, c_sig, ALU.mult).then_inc(s_cact, 1)
            dve.wait_ge(s_brow, 16)
            v.tensor_copy(brow[:, 0:P - 1], brow[:, P - 1:P].to_broadcast([HEADS, P - 1])).then_inc(s_bfill, 1)
            dve.wait_ge(s_cact, 2)

            def modulation(n):
                dve.wait_ge(s_accb[n % 2], 16 * (n // 2 + 1))
                for half in range(2):
                    pg = page_of("ada", n, half)
                    page_landed(dve, pg)
                    for k in range(4):
                        kk = 4 * half + k
                        ins = v.scalar_tensor_tensor(out=acc[:, n % 2, :], in0=page_k(pg, k), scalar=c_act[:, kk:kk + 1],
                                                     in1=acc[:, n % 2, :], op0=ALU.mult, op1=ALU.add)
                        if k < 3:
                            link(ins)
                        else:
                            ins.then_inc(s_dve_page, 1)
                            dve.wait_ge(s_dve_page, 2 * n + half + 1)

            def mod_bank(n):
                return po[:, 2:4, :] if n % 2 == 0 else po[:, 0:2, :]

            def flat2(ap):
                return ap.rearrange("p b n -> p (b n)")

            modulation(0)
            modulation(1)
            dve.wait_ge(s_ssx, 1)
            link(v.reciprocal(rstd[:, 0:2], rms[:, 0:2]))
            dve.wait_ge(s_adasum, 2)
            dve.wait_ge(s_gain[0], 16)
            link(v.scalar_tensor_tensor(out=scale, in0=flat2(mod_bank(1)), scalar=1.0, in1=scale,
                                        op0=ALU.add, op1=ALU.mult))
            for t in range(TT):
                v.scalar_tensor_tensor(out=h_sb[:, t, :], in0=x_sb[:, t, :], scalar=rstd[:, t:t + 1], in1=scale,
                                       op0=ALU.mult, op1=ALU.mult).then_inc(s_h0, 1)
            modulation(2)
            dve.wait_ge(s_adasum, 3)
            dve.wait_ge(s_gain[1], 16)
            v.tensor_tensor(gain1, gain1, flat2(mod_bank(2)), ALU.mult).then_inc(s_mod_v, 1)
            modulation(3)
            modulation(4)
            dve.wait_ge(s_adasum, 5)
            dve.wait_ge(s_gain[2], 16)
            v.scalar_tensor_tensor(out=scale, in0=flat2(mod_bank(4)), scalar=1.0, in1=scale,
                                   op0=ALU.add, op1=ALU.mult).then_inc(s_mod_v, 1)
            modulation(5)
            dve.wait_ge(s_adasum, 6)
            dve.wait_ge(s_gain[3], 16)
            v.tensor_tensor(gain2[:], gain2[:], flat2(mod_bank(5)), ALU.mult).then_inc(s_mod_v, 1)

            dve.wait_ge(s_projev, 12)
            for t in range(TT):
                link(v.bn_stats(stats[:, t, :], vv[:, t, :]))
                v.bn_aggr(meanvar[:, t, :], stats[:, t, :]).then_inc(s_mv, 1)
            dve.wait_ge(s_lnsq, 1)
            link(v.reciprocal(rstd[:, 2:4], rms[:, 2:4]))
            for t in range(TT):
                v.tensor_scalar(vv[:, t, :], vv[:, t, :], meanvar[:, t, 0:1], rstd[:, 2 + t:3 + t],
                                ALU.subtract, ALU.mult).then_inc(s_lnn, 1)
            dve.wait_ge(s_bmask, 1)
            dve.wait_ge(s_bs, 32)
            dve.wait_ge(s_projev, 14)
            for m in range(KA):
                dve.wait_ge(s_sgu, m // 2 + 1)
                src = po[:, 2 + m // 2, (m % 2) * TOK:(m % 2 + 1) * TOK].rearrange("p (b t) -> p b t", b=TT)
                dst = prob[:, 0, 0:TOK].rearrange("p (b t) -> p b t", b=TT)
                link(v.tensor_tensor(dst, src, bsb[:, m:m + 1, :].to_broadcast([P, TT, P]), ALU.add))
                ins = v.tensor_tensor(ybT[:, m, :], ybT[:, m, :], prob[:, 0, 0:TOK], ALU.mult)
                ins.then_inc(s_yb, 1)
                dve.wait_ge(s_yb, m + 1)

            def scores_bias(h):
                dve.wait_ge(s_score, h + 1)
                if h >= 2:
                    dve.wait_ge(s_pT, h - 1)
                v.tensor_tensor(prob[:, h % 2, 0:P], po[:, h % 2, 0:P], bias[:, h, P:TOK], ALU.add)
                link(v.tensor_tensor(prob[:, h % 2, P:BW], po[:, h % 2, P:BW], bias[:, h, :], ALU.add))
                v.tensor_reduce(nmax[:, h % 2, 0:1], prob[:, h % 2, 0:P], AX.X, ALU.max, negate=True)
                v.tensor_reduce(nmax[:, h % 2, 1:2], prob[:, h % 2, P:BW], AX.X, ALU.max,
                                negate=True).then_inc(s_soft, 1)

            def normalise(h):
                dve.wait_ge(s_exp, h + 1)
                link(v.reciprocal(prc[:, h % 2, :], psm[:, h % 2, :]))
                v.tensor_scalar(prob[:, h % 2, 0:P], prob[:, h % 2, 0:P], prc[:, h % 2, 0:1], None, ALU.mult)
                v.tensor_scalar(prob[:, h % 2, P:BW], prob[:, h % 2, P:BW], prc[:, h % 2, 1:2], None,
                                ALU.mult).then_inc(s_prob, 1)

            def heads_out(m):
                dve.wait_ge(s_pv, 2 * m + 2)
                v.tensor_copy(yaT[:, m, :], po[:, 3, 0:TOK]).then_inc(s_ya, 1)

            scores_bias(0)
            for h in range(HEADS):
                if h >= 2 and h % 2 == 0:
                    heads_out(h // 2 - 1)
                if h + 1 < HEADS:
                    scores_bias(h + 1)
                normalise(h)
            heads_out(KA - 1)

            for m in range(KD):
                dve.wait_ge(s_br, m + 1)
                v.tensor_tensor(gates[:, m, :], pp[:, m % 4, 0:TOK], gates[:, m, :], ALU.mult)
                v.tensor_tensor(gates[:, KD + m, :], pp[:, m % 4, TOK:2 * TOK], gates[:, KD + m, :],
                                ALU.mult).then_inc(s_mg, 1)

            dve.wait_ge(s_mod_a, 2)
            for t in range(TT):
                dve.wait_ge(s_ssy, t + 1)
                link(v.reciprocal(rstd[:, 4 + t:5 + t], rms[:, 4 + t:5 + t]))
                y = po[:, 2 * t:2 * t + 2, :].rearrange("p b n -> p (b n)")
                link(v.scalar_tensor_tensor(out=h_sb[:, t, :], in0=y, scalar=rstd[:, 4 + t:5 + t], in1=gain1,
                                            op0=ALU.mult, op1=ALU.mult))
                v.tensor_tensor(x_sb[:, t, :], x_sb[:, t, :], h_sb[:, t, :], ALU.add).then_inc(s_x1, 1)
                dve.wait_ge(s_ssx1, t + 1)
                link(v.reciprocal(rstd[:, 6 + t:7 + t], rms[:, 6 + t:7 + t]))
                link(v.scalar_tensor_tensor(out=h_sb[:, t, :], in0=x_sb[:, t, :], scalar=rstd[:, 6 + t:7 + t],
                                            in1=scale, op0=ALU.mult, op1=ALU.mult))
                v.tensor_tensor(h_sb[:, t, :], h_sb[:, t, :], shift, ALU.add).then_inc(s_h2, 1)

            dve.wait_ge(s_wr, 32)
            for t in range(TT):
                dve.wait_ge(s_lg, t + 1)
                link(v.tensor_tensor(logit[:, t, :], pp[:, 2 + t, 0:NEXP], b_rt, ALU.add))
                link(v.max(top8[:, t, :], logit[:, t, :]))
            v.tensor_scalar(r1[:, 0:2], top8[:, :, 0], -1.0, None, ALU.mult).then_inc(s_ngm, 1)
            for t in range(TT):
                fourth = top8[:, t, TOPK - 1:TOPK]
                v.tensor_scalar(above[:, t, :], logit[:, t, :], fourth, None, ALU.is_gt)
                link(v.tensor_scalar(equal[:, t, :], logit[:, t, :], fourth, None, ALU.is_equal))
            link(v.tensor_reduce(r1[:, 2:4], above, AX.X, ALU.add))
            link(v.tensor_scalar(r1[:, 2:4], r1[:, 2:4], -1.0, float(TOPK), ALU.mult, ALU.add))
            for t in range(TT):
                link(v.tensor_tensor_scan(upto[:, t, :], ones[:, 0:NEXP], equal[:, t, :], 0.0, ALU.mult, ALU.add))
                link(v.scalar_tensor_tensor(out=equal[:, t, :], in0=upto[:, t, :], scalar=r1[:, 2 + t:3 + t],
                                            in1=equal[:, t, :], op0=ALU.is_le, op1=ALU.mult))
            v.tensor_tensor(chosen, above, equal, ALU.add).then_inc(s_chosen, 1)
            dve.wait_ge(s_chosen, 1)
            dve.wait_ge(s_ex, 1)
            link(v.tensor_tensor(expo, expo, chosen, ALU.mult))
            link(v.tensor_reduce(r1[:, 4:6], expo, AX.X, ALU.add))
            link(v.reciprocal(r1[:, 6:8], r1[:, 4:6]))
            for t in range(TT):
                ins = v.tensor_scalar(gate_tab[:, t, :], expo[:, t, :], r1[:, 6 + t:7 + t], None, ALU.mult)
            link(ins)
            dve.wait_ge(s_const, 5)
            dve.wait_ge(s_rank, 1)
            counts = pp[:, 0, 2 * NEXP:3 * NEXP]
            link(v.tensor_copy(nblk_f, counts))
            for m in range(7):
                ins = v.tensor_scalar(cmp7[:, :, m], nblk_f, float(TB * (m + 1)), None, ALU.is_gt)
            link(ins)
            link(v.tensor_reduce(nblk_f, cmp7, AX.X, ALU.add))
            v.tensor_scalar(nblk_i[:], nblk_f, 1.0, None, ALU.add)
            link(v.scalar_tensor_tensor(out=rank, in0=pp[:, 0, 0:2 * NEXP].rearrange("p (t e) -> p t e", t=TT),
                                        scalar=1.0, in1=chosen, op0=ALU.add, op1=ALU.mult))
            for b in range(NBLK):
                ins = v.tensor_scalar(rank_tab[:, :, b, :], rank, -1.0 - TB * b, None, ALU.add)
            ins.then_inc(s_tabs, 1)
            dve.wait_ge(s_tabs, 1)
            dve.wait_ge(s_sgp, 1)
            v.memset(y_sb, 0.0)
            v.memset(selgT, 0.0).then_inc(s_ysb, 1)

            item = dve.alloc_register("dve_item")
            dve.reg_mov(item, 0)
            with dve.Fori(0, NEXP) as e:
                nb = dve.value_load(nblk_i[0:1, bass.ds(e, 1)], min_val=1, max_val=NBLK)
                with dve.Fori(0, nb) as b:
                    dve.reg_add(item, item, 1)
                    it = dve.snap(item, min_val=1, max_val=NEXP * NBLK)
                    dve.wait_ge(s_sgp, it)
                    for t in range(TT):
                        rk = rank_tab[:, t, bass.ds(b, 1), bass.ds(e, 1)]
                        gt = gate_tab[:, t, bass.ds(e, 1)]
                        v.tensor_scalar(sel[:, t, :], iota[:, 0, :], rk, None, ALU.is_equal)
                        ins = v.tensor_scalar(selg[:, t, :, :], iota[:], rk, gt, ALU.is_equal, ALU.mult)
                    ins.then_inc(s_sel, 1)
                    dve.wait_ge(s_gu, it)
                    v.tensor_scalar(glu, pp[:, 0, 0:QF], LIMIT, None, ALU.min).then_inc(s_glu, 1)
                    v.tensor_scalar(lin, pp[:, 0, QF:2 * QF], LIMIT, -LIMIT, ALU.min, ALU.max).then_inc(s_lin, 1)
                    dve.wait_ge(s_lin, it)
                    v.scalar_tensor_tensor(out=tmp, in0=lin, scalar=1.0, in1=glu, op0=ALU.add,
                                           op1=ALU.mult).then_inc(s_tmp, 1)
                    dve.wait_ge(s_tmp, it)
                    dve.wait_ge(s_sig, it)
                    v.tensor_tensor(act_sb.rearrange("p h f -> p (h f)"), tmp, sig, ALU.mult).then_inc(s_actv, 1)

            dve.wait_ge(s_ssf, 1)
            link(v.reciprocal(rstd[:, 0:2], rms[:, 0:2]))
            dve.wait_ge(s_x1b, 16)
            for t in range(TT):
                y = po[:, 2 * t:2 * t + 2, :].rearrange("p b n -> p (b n)")
                link(v.scalar_tensor_tensor(out=y_out[:, t, :], in0=y, scalar=rstd[:, t:t + 1], in1=gain2[:],
                                            op0=ALU.mult, op1=ALU.mult))
                v.tensor_tensor(y_out[:, t, :], y_out[:, t, :], x1_back[:, t, :], ALU.add).then_inc(s_yo, 1)

        @block.tensor
        def _(pe):
            t_ = nc.tensor
            pe.wait_ge(s_const, 1)
            pe.wait_ge(s_c, 16)
            t_.transpose(pp[:, 0, 0:KD], c8, ident[0:8, 0:8]).then_inc(s_cT, 1)
            pe.wait_ge(s_ws, 16)
            for b in range(2):
                for i in range(4):
                    mm = t_.transpose(po[:, b, i * P:(i + 1) * P], ws[:, 4 * b + i, :], ident[:])
                mm.then_inc(s_wsp, 1)

            def modulation_sum(n):
                if n == 0:
                    pe.wait_ge(s_pool, 2)
                elif n == 1:
                    pe.wait_ge(s_wsT, 2)
                elif n == 2:
                    pe.wait_ge(s_mod_a, 1)
                elif n == 3:
                    pe.wait_ge(s_h0, 1)
                elif n == 4:
                    pe.wait_ge(s_mod_v, 1)
                else:
                    pe.wait_ge(s_mod_a, 2)
                pe.wait_ge(s_dve_page, 2 * n + 2)
                for half in range(2):
                    mm = t_.matmul(po[:, 2 * (1 - n % 2) + half, :], ones[:], acc[:, n % 2, half * 512:(half + 1) * 512],
                                   start=True, stop=True)
                mm.then_inc(s_adasum, 1)

            modulation_sum(0)
            modulation_sum(1)

            bank = 0

            def next_bank():
                nonlocal bank
                if bank >= 4:
                    pe.wait_ge(s_projev, bank - 3)
                bank += 1
                return pp[:, (bank - 1) % 4, :]

            for t in range(TT):
                pe.wait_ge(s_h, t + 1)
                for q in range(2):
                    ps = next_bank()
                    for i in range(4):
                        mm = t_.transpose(ps[:, i * P:(i + 1) * P], h_sb[:, t, (4 * q + i) * P:(4 * q + i + 1) * P],
                                          ident[:])
                    mm.then_inc(s_proj, 1)
            pe.wait_ge(s_projev, 4)

            def page_T(name):
                pg = page_of(name)
                page_landed(pe, pg)
                for b in range(2):
                    ps = next_bank()
                    for i in range(2):
                        m = 2 * b + i
                        for k in range(KD):
                            mm = t_.matmul(ps[:, i * TOK:(i + 1) * TOK], page_k(pg, k)[:, m * P:(m + 1) * P],
                                           hT[:, k, :], start=(k == 0), stop=(k == KD - 1))
                    mm.then_inc(s_proj, 1)

            def page_rows(name):
                pg = page_of(name)
                page_landed(pe, pg)
                for t in range(TT):
                    ps = next_bank()
                    for k in range(KD):
                        mm = t_.matmul(ps, hT[:, k, t * P:(t + 1) * P], page_k(pg, k), start=(k == 0),
                                       stop=(k == KD - 1))
                    mm.then_inc(s_proj, 1)

            page_T("q")
            modulation_sum(2)
            page_T("k")
            modulation_sum(3)
            page_rows("v")
            modulation_sum(4)
            page_rows("vv")
            modulation_sum(5)
            page_T("u")

            pe.wait_ge(s_lnd, TT)
            pe.wait_ge(s_wsm, 1)
            pe.wait_ge(s_mod_v, 2)
            for m in range(KA):
                for r in range(2):
                    for b in range(TT):
                        g = 2 * m + r
                        col = (m % 2) * TOK + b * P
                        mm = t_.matmul(po[HD * r:HD * r + HD, 2 + m // 2, col:col + P], vv[:, b, g * HD:(g + 1) * HD],
                                       wsT[:, g, :], start=True, stop=True)
                if m % 2:
                    mm.then_inc(s_sgu, 1)

            def scores(h):
                m, r = h // 2, HD * (h % 2)
                if h == 0:
                    pe.wait_ge(s_projev, 8)
                    pe.wait_ge(s_mod_v, 3)
                if h >= 2:
                    pe.wait_ge(s_soft, h - 1)
                t_.matmul(po[:, h % 2, 0:P], qT[r:r + HD, m, 0:P], kT[r:r + HD, m, 0:P], start=True, stop=True)
                t_.matmul(po[:, h % 2, P:BW], qT[r:r + HD, m, P:TOK], kT[r:r + HD, m, :], start=True,
                          stop=True).then_inc(s_score, 1)

            scores(0)
            scores(1)
            for h in range(HEADS):
                pg = page_of("gate", h // 2)
                if h % 2 == 0:
                    page_landed(pe, pg)
                ps = next_bank()
                for i in range(2):
                    m = 2 * (h % 2) + i
                    for k in range(KD):
                        mm = t_.matmul(ps[:, i * TOK:(i + 1) * TOK], page_k(pg, k)[:, m * P:(m + 1) * P], hT[:, k, :],
                                       start=(k == 0), stop=(k == KD - 1))
                mm.then_inc(s_proj, 1)
                pe.wait_ge(s_prob, h + 1)
                if h == 0:
                    pe.wait_ge(s_yb, KA)
                for i in range(3):
                    mm = t_.transpose(po[:, 2, i * P:(i + 1) * P], prob[:, h % 2, i * P:(i + 1) * P], ident[:])
                mm.then_inc(s_pT, 1)
                pe.wait_ge(s_pTev, h + 1)
                if h >= 2 and h % 2 == 0:
                    pe.wait_ge(s_ya, h // 2)
                r, col = HD * (h % 2), 0
                t_.matmul(po[r:r + HD, 3, col:col + P], v_sb[:, 0, h * HD:(h + 1) * HD], probT[:, 0:P], start=True,
                          stop=True)
                for b in range(TT):
                    mm = t_.matmul(po[r:r + HD, 3, col + P:col + TOK], v_sb[:, b, h * HD:(h + 1) * HD],
                                   probT[:, (1 + b) * P:(2 + b) * P], start=(b == 0), stop=(b == 1))
                mm.then_inc(s_pv, 1)
                if h + 2 < HEADS:
                    scores(h + 2)

            pe.wait_ge(s_ya, KA)
            pe.wait_ge(s_projev, bank)
            pga, pgb = page_of("ba"), page_of("bb")
            page_landed(pe, pga)
            page_landed(pe, pgb)
            for m in range(KD):
                if m >= 4:
                    pe.wait_ge(s_mg, m - 3)
                for half, (pg, src) in enumerate(((pga, yaT), (pgb, ybT))):
                    for k in range(KA):
                        mm = t_.matmul(pp[:, m % 4, half * TOK:(half + 1) * TOK], page_k(pg, k)[:, m * P:(m + 1) * P],
                                       src[:, k, :], start=(k == 0), stop=(k == KA - 1))
                mm.then_inc(s_br, 1)

            for i in range(2):
                page_landed(pe, page_of("wo", i))
            for t in range(TT):
                for k in range(KD):
                    if t == 0:
                        pe.wait_ge(s_merged, k + 1)
                    for half in range(2):
                        mm = t_.matmul(po[:, 2 * t + half, :], mergedT[:, k, t * P:(t + 1) * P],
                                       page_k(page_of("wo", k // 4), k % 4)[:, half * 512:(half + 1) * 512],
                                       start=(k == 0), stop=(k == KD - 1))
                mm.then_inc(s_wo, 1)

            pe.wait_ge(s_wr, 32)
            pe.wait_ge(s_mg, KD)
            for t in range(TT):
                pe.wait_ge(s_h2, t + 1)
                for q in range(2):
                    if t:
                        pe.wait_ge(s_h2T, q + 1)
                    for i in range(4):
                        mm = t_.transpose(pp[:, q, i * P:(i + 1) * P], h_sb[:, t, (4 * q + i) * P:(4 * q + i + 1) * P],
                                          ident[:])
                    mm.then_inc(s_h2p, 1)
                for k in range(KD):
                    if k % 4 == 0:
                        pe.wait_ge(s_h2T, 2 * t + k // 4 + 1)
                    mm = t_.matmul(pp[:, 2 + t, 0:NEXP], h2T[:, k, t * P:(t + 1) * P], wr[:, k, :], start=(k == 0),
                                   stop=(k == KD - 1))
                mm.then_inc(s_lg, 1)

            pe.wait_ge(s_const, 5)
            pe.wait_ge(s_chosen, 1)
            t_.matmul(pp[:, 0, 0:NEXP], before[:], chosen[:, 0, :], start=True, stop=True)
            for col, second in ((NEXP, before), (2 * NEXP, ones)):
                t_.matmul(pp[:, 0, col:col + NEXP], ones[:], chosen[:, 0, :], start=True, stop=False)
                mm = t_.matmul(pp[:, 0, col:col + NEXP], second[:], chosen[:, 1, :], start=False, stop=True)
            mm.then_inc(s_rank, 1)
            pe.wait_ge(s_tabs, 1)
            for t in range(TT):
                mm = t_.transpose(pp[0:NEXP, 1, t * P:(t + 1) * P], gate_tab[:, t, :], ident[:])
            mm.then_inc(s_gT, 1)
            pe.wait_ge(s_gTev, 1)
            pe.wait_ge(s_bdl, 16)
            pe.wait_ge(s_h2, TT)
            for t in range(TT):
                for half in range(2):
                    mm = t_.matmul(po[:, 2 * t + half, :], gateT[:, t, :], bd_sb[:, half * 512:(half + 1) * 512],
                                   start=True, stop=False, skip_group_check=True)
            mm.then_inc(s_sgp, 1)

            def combine(it, final=False):
                pe.wait_ge(s_ysb, it)
                for rnd in range(2):
                    for j in range(CT):
                        half = j // 2
                        t = (j + rnd) % 2
                        col = (j % 2) * QF
                        mm = t_.matmul(po[:, 2 * t + half, col:col + QF], selgT[j * TB:(j + 1) * TB, t, :],
                                       y_sb[j * TB:(j + 1) * TB, :], start=False, stop=final and rnd == 1,
                                       skip_group_check=True)
                    if rnd == 0:
                        mm.then_inc(s_half, 1)
                        pe.wait_ge(s_half, it)
                return mm

            item = pe.alloc_register("pe_item")
            pe.reg_mov(item, 0)
            pe.wait_ge(s_sgp, 1)
            with pe.Fori(0, NEXP // 2) as i:
                for slot in range(2):
                    nb = pe.value_load(nblk_i[0:1, bass.ds(i * 2 + slot, 1)], min_val=1, max_val=NBLK)
                    with pe.Fori(0, nb) as b:
                        pe.reg_add(item, item, 1)
                        it = pe.snap(item, min_val=1, max_val=NEXP * NBLK)
                        landed = i * 16 + 16
                        pe.wait_ge(s_sel, it)
                        for k in range(KD):
                            for t in range(TT):
                                mm = t_.matmul(pp[:, 2, k * TB:(k + 1) * TB], h_sb[:, t, k * P:(k + 1) * P],
                                               sel[:, t, :], start=(t == 0), stop=(t == TT - 1))
                        mm.then_inc(s_hg, 1)
                        combine(it)
                        pe.wait_ge(s_bgu[slot], landed)
                        for t in range(TT):
                            mm = t_.transpose(pp[:, 3, 256 + t * P:256 + (t + 1) * P],
                                              selg[:, t, :, :].rearrange("p c j -> p (c j)"), ident[:])
                        mm.then_inc(s_sgp, 1)
                        for half in range(2):
                            for j in range(CT):
                                t_.matmul(pp[j * TB:(j + 1) * TB, 0, half * QF:(half + 1) * QF],
                                          pick8[:, half * CT + j, :], bgu[:, slot, :], start=(half == 0), stop=False,
                                          skip_group_check=True)
                        pe.wait_ge(s_hgT, it)
                        for k in range(KD):
                            if k % 2 == 0:
                                pe.wait_ge(s_gup[slot][k // 2], landed)
                            for j in range(CT):
                                mm = t_.matmul(pp[j * TB:(j + 1) * TB, 0, :].rearrange("p (s f) -> p s f", s=2),
                                               hgT[:, k, :], gu_w[slot][:, k, :, j * QF:(j + 1) * QF], start=False,
                                               stop=(k == KD - 1), skip_group_check=True)
                        mm.then_inc(s_gu, 1)
                        pe.wait_ge(s_actv, it)
                        for hh in range(2):
                            mm = t_.transpose(pp[:, 3, hh * P:(hh + 1) * P], act_sb[:, hh, :], ident[:])
                        mm.then_inc(s_aT, 1)
                        pe.wait_ge(s_aTev, it)
                        for cf in range(KD):
                            if cf == 0:
                                pe.wait_ge(s_dlo[slot], landed)
                            if cf == 4:
                                pe.wait_ge(s_dhi, i * 32 + 16 * (slot + 1))
                            w = dlo_w[slot][:, cf, :] if cf < 4 else dhi_w[:, cf - 4, :]
                            for j in range(CT):
                                mm = t_.matmul(pp[j * TB:(j + 1) * TB, 1, 0:QF],
                                               actT[:, cf % 2, (cf // 2) * TB:(cf // 2 + 1) * TB],
                                               w[:, j * QF:(j + 1) * QF], start=(cf == 0), stop=(cf == KD - 1))
                        mm.then_inc(s_y, 1)
            pe.reg_add(item, item, 1)
            combine(pe.snap(item, min_val=1, max_val=NEXP * NBLK + 1), final=True).then_inc(s_fin, 1)


_INS = ["x", "c", "w_ada", "b_ada", "g_pre_mix", "g_post_mix", "w_in", "rel_bias", "sgu_ln_g", "sgu_ln_b",
        "w_spatial", "b_spatial", "w_branch_a", "w_branch_b", "w_gate", "b_gate", "w_out", "g_pre_ffn",
        "g_post_ffn", "w_router", "b_router", "w_gate_up", "b_gate_up", "w_down", "b_down"]
_OUTS = [((1, TOK, D), "float32")]


def kernel(**inputs):
    import numpy as _np
    import concourse.bacc as _bacc
    from concourse import mybir as _mybir
    from concourse.bass_utils import run_bass_kernel_spmd as _run

    nc = _bacc.Bacc("TRN2", target_bir_lowering=False, num_devices=1)
    arrays, args = {}, []
    for name in _INS:
        a = _np.asarray(inputs[name])
        if name == "rel_bias":
            a = a[:, :, ::-1]
        a = _np.ascontiguousarray(a)
        arrays[f"in_{name}_dram"] = a
        args.append(nc.dram_tensor(f"in_{name}_dram", a.shape, _mybir.dt.from_np(a.dtype), kind="ExternalInput").ap())
    for i, (shape, dtype) in enumerate(_OUTS):
        dt = _mybir.dt.from_np(_np.dtype(dtype))
        args.append(nc.dram_tensor(f"out_{i}_dram", shape, dt, kind="ExternalOutput").ap())
    block_program(nc, *args)
    r = _run(nc, [arrays], core_ids=[0])
    return r.results[0]["out_0_dram"]
```

```python
from contextlib import ExitStack

import concourse.bass as bass
from concourse import mybir

ALU = mybir.AluOpType
ACT = mybir.ActivationFunctionType
F32 = mybir.dt.float32
I32 = mybir.dt.int32
BF16 = mybir.dt.bfloat16
AX = mybir.AxisListType

P = 128
TOK, D = 256, 1024
TT = TOK // P
KD = D // P
AW = 512
KA = AW // P
HEADS, HD = 8, 64
NREL = 257
GROUPS = 8
NMOD = 6
NEXP, TOPK = 32, 4
F = 1024
TB = 32
CT = P // TB
QF = F // CT
NBLK = TOK // TB
QH = QF // 2
LIMIT, ALPHA, EPS = 7.0, 1.702, 1e-6
NEG = -1e30
BW = 3 * P
PAGE = 4096
RING = 5

PAGES = [("dve", "ada", 0, 0), ("dve", "ada", 0, 1), ("dve", "ada", 1, 0), ("dve", "ada", 1, 1)]
for _n, _name in enumerate(("q", "k", "v", "vv")):
    PAGES += [("pe", _name, 0, 0), ("dve", "ada", _n + 2, 0), ("dve", "ada", _n + 2, 1)]
PAGES += [("pe", "u", 0, 0)] + [("pe", "gate", _n, 0) for _n in range(4)]
PAGES += [("pe", "ba", 0, 0), ("pe", "bb", 0, 0), ("pe", "wo", 0, 0), ("pe", "wo", 1, 0)]
IN_COL = {"q": 0, "k": AW, "v": 2 * AW, "u": 3 * AW, "vv": 4 * AW}


def page_of(name, part=0, half=0):
    return [n for n, pg in enumerate(PAGES) if pg[1:] == (name, part, half)][0]


def consumed(n):
    who, name, i, _ = PAGES[n]
    if who == "dve":
        return "dve_page", sum(1 for pg in PAGES[:n + 1] if pg[0] == "dve")
    if name in ("ba", "bb"):
        return "branch", KD
    if name == "wo":
        return "wo", TT
    return "proj", 4 + 2 * sum(1 for pg in PAGES[:n + 1] if pg[0] == "pe") + (0 if name == "q" else 2)


def block_program(nc, x, c, w_ada, b_ada, g_pre_mix, g_post_mix, w_in, rel_rev, sgu_ln_g, sgu_ln_b,
                  w_spatial, b_spatial, w_branch_a, w_branch_b, w_gate, b_gate, w_out, g_pre_ffn,
                  g_post_ffn, w_router, b_router, w_gate_up, b_gate_up, w_down, b_down, out):
    with ExitStack() as ctx:
        def sb(name, shape, dt=F32):
            return ctx.enter_context(nc.sbuf_tensor(name, shape, dt))

        def psum(name, shape):
            return ctx.enter_context(nc.psum_tensor(name, shape, F32))

        def sem(name):
            return ctx.enter_context(nc.semaphore(name))

        arena = sb("arena", [P, 11 * PAGE])

        def page(n, cols=PAGE):
            return arena[:, n * PAGE:n * PAGE + cols]

        def part(start, cols):
            return arena[:, start:start + cols]

        at5 = 5 * PAGE
        acc = part(at5, 2 * D).rearrange("p (b d) -> p b d", b=2)
        qT = part(at5 + 2048, KA * TOK).rearrange("p (m t) -> p m t", m=KA)
        kT = part(at5 + 3072, KA * TOK).rearrange("p (m t) -> p m t", m=KA)
        v_sb = part(at5 + 4096, TT * AW).rearrange("p (t w) -> p t w", t=TT)
        vv = part(at5 + 5120, TT * AW).rearrange("p (t w) -> p t w", t=TT)
        bias = part(at5 + 6144, HEADS * TOK).rearrange("p (h k) -> p h k", h=HEADS)
        wsT = part(at5 + 8192, GROUPS * P).rearrange("p (g t) -> p g t", g=GROUPS)
        ws = part(at5 + 9216, GROUPS * P).rearrange("p (g s) -> p g s", g=GROUPS)
        bsb = part(at5 + 10240, KA * P).rearrange("p (m t) -> p m t", m=KA)
        ybT = part(at5 + 10752, KA * TOK).rearrange("p (m t) -> p m t", m=KA)
        at8 = 8 * PAGE
        x_sb = part(at8, TT * D).rearrange("p (t d) -> p t d", t=TT)
        hT = part(at8 + 2048, KD * TOK).rearrange("p (k t) -> p k t", k=KD)
        mergedT = hT
        gates = part(at8 + 4096, 2 * KD * TOK).rearrange("p (m t) -> p m t", m=2 * KD)
        h2T = part(at8 + 4096, KD * TOK).rearrange("p (k t) -> p k t", k=KD)
        shift = part(at8 + 8192, D)
        scale = part(at8 + 9216, D)
        gain1 = part(at8 + 10240, D)
        yaT = part(at8 + 11264, KA * TOK).rearrange("p (m t) -> p m t", m=KA)

        squares = part(at8 + 6144, D)
        bm = part(at8 + 4096, D)[0:NMOD, :]
        cb_rows = part(at8 + 5120, P)[0:KD + 2 * KD, :]

        gu_w = [part(b * 4 * PAGE, 4 * PAGE).rearrange("p (k s f) -> p k s f", k=KD, s=2) for b in range(2)]
        dlo_w = [page(8 + b).rearrange("p (k d) -> p k d", k=4) for b in range(2)]
        dhi_w = page(10).rearrange("p (k d) -> p k d", k=4)
        x1_back = page(0, TT * D).rearrange("p (t d) -> p t d", t=TT)
        y_out = page(1, TT * D).rearrange("p (t d) -> p t d", t=TT)
        bd_back = page(2, D)[0:NEXP, :]

        h_sb = sb("h_sb", [P, TT, D])
        gain2 = sb("gain2", [P, D])
        ident = sb("ident", [P, P])
        ones = sb("ones", [P, P])
        iota = sb("iota", [P, TB])
        rank_tab = sb("rank_tab", [P, TT, NBLK, NEXP])
        gate_tab = sb("gate_tab", [P, TT, NEXP])
        nblk_i = sb("nblk_i", [P, NEXP], I32)
        bgu = sb("bgu", [CT, 2, 2 * QF])
        pick = sb("pick", [CT, CT, TB])
        work = sb("work", [P, 2624])
        prob = work[:, 0:2 * BW].rearrange("p (b k) -> p b k", b=2)
        probT = work[:, 768:768 + BW]
        ln_g = work[:, 1152:1152 + AW]
        ln_b = work[:, 1664:1664 + AW]
        wr = work[:, 2176:2176 + KD * NEXP].rearrange("p (k e) -> p k e", k=KD)
        before = work[:, 2432:2432 + P]
        brow = work[0:HEADS, 0:BW]
        sel = work[:, 0:64].rearrange("p (t j) -> p t j", t=TT)
        selg = work[:, 64:320].rearrange("p (t c j) -> p t c j", t=TT, c=CT)
        turned = work[:, 320:832]
        hgT = turned[:, 0:256].rearrange("p (h n) -> p h n", h=2)
        selgT = turned[:, 256:512].rearrange("p (t n) -> p t n", t=TT)
        hg = work[:, 832:1088].rearrange("p (h n) -> p h n", h=2)
        gateT = work[0:NEXP, 832:1088].rearrange("p (t n) -> p t n", t=TT)
        y_sb = work[:, 1088:1344]
        sig = work[:, 1344:1600].rearrange("p (h n) -> p h n", h=2)
        lin = work[:, 1600:1856].rearrange("p (h n) -> p h n", h=2)
        act_sb = work[:, 1856:2112].rearrange("p (h n) -> p h n", h=2)
        glu = work[:, 2112:2368].rearrange("p (h n) -> p h n", h=2)
        actT = work[:, 2368:2624].rearrange("p (h n) -> p h n", h=2)
        chosen = work[:, 0:64].rearrange("p (t e) -> p t e", t=TT)
        expo = work[:, 64:128].rearrange("p (t e) -> p t e", t=TT)
        rank = work[:, 128:192].rearrange("p (t e) -> p t e", t=TT)
        cmp7 = work[:, 192:192 + 7 * NEXP].rearrange("p (e m) -> p e m", m=7)
        nblk_f = work[:, 448:480]
        upto = work[:, 480:544].rearrange("p (t e) -> p t e", t=TT)
        small = sb("small", [P, 352])
        c_act = small[:, 0:8]
        c_sig = small[:, 8:16]
        cb_col = small[:, 16:40]
        c_col = small[:, 16:24]
        bg_col = small[:, 24:40]
        ssq = small[:, 40:52]
        rms = small[:, 52:60]
        rstd = small[:, 60:68]
        part_ms = small[:, 68:72]
        stats = small[:, 72:84].rearrange("p (t s) -> p t s", t=TT)
        meanvar = small[:, 84:88].rearrange("p (t s) -> p t s", t=TT)
        nmax = small[:, 88:92].rearrange("p (b s) -> p b s", b=2)
        psm = small[:, 92:96].rearrange("p (b s) -> p b s", b=2)
        prc = small[:, 96:100].rearrange("p (b s) -> p b s", b=2)
        eps_col = small[:, 100:101]
        b_rt = small[:, 104:136]
        logit = small[:, 136:200].rearrange("p (t e) -> p t e", t=TT)
        top8 = small[:, 200:216].rearrange("p (t e) -> p t e", t=TT)
        above = small[:, 216:280].rearrange("p (t e) -> p t e", t=TT)
        equal = small[:, 280:344].rearrange("p (t e) -> p t e", t=TT)
        r1 = small[:, 344:352]

        UP, TOKS, TURN = (0, 1), 2, 3
        pp = psum("pp", [P, 4, 512])
        po = psum("po", [P, 4, 512])

        bias_rows = nc.dram_tensor("bias_rows", [HEADS, P, BW], F32)
        x1_dram = nc.dram_tensor("x1_dram", [P, TT, D], F32)

        s_page = [sem(f"s_page{i}") for i in range(RING)]
        s_dve_page = sem("s_dve_page")
        s_x, s_c, s_ws, s_bm = sem("s_x"), sem("s_c"), sem("s_ws"), sem("s_bm")
        s_ln, s_bs, s_wr = sem("s_ln"), sem("s_bs"), sem("s_wr")
        s_brow, s_bfill, s_brows, s_bias, s_bmask = (sem("s_brow"), sem("s_bfill"), sem("s_brows"),
                                                     sem("s_bias"), sem("s_bmask"))
        s_gain = [sem(f"s_gain{i}") for i in range(4)]
        s_const, s_pool = sem("s_const"), sem("s_pool")
        s_cT, s_csig, s_cact = sem("s_cT"), sem("s_csig"), sem("s_cact")
        s_adasum, s_mod_a, s_mod_v = sem("s_adasum"), sem("s_mod_a"), sem("s_mod_v")
        s_wsm = sem("s_wsm")
        s_ssx, s_scale, s_h = sem("s_ssx"), sem("s_scale"), sem("s_h")
        s_proj, s_projev = sem("s_proj"), sem("s_projev")
        s_mv, s_lnsq, s_lnn, s_lng, s_lnd = sem("s_mv"), sem("s_lnsq"), sem("s_lnn"), sem("s_lng"), sem("s_lnd")
        s_sgu, s_yb = sem("s_sgu"), sem("s_yb")
        s_score, s_soft, s_exp, s_prob = sem("s_score"), sem("s_soft"), sem("s_exp"), sem("s_prob")
        s_pT, s_pTev, s_pv, s_ya = sem("s_pT"), sem("s_pTev"), sem("s_pv"), sem("s_ya")
        s_br, s_mg, s_merged = sem("s_br"), sem("s_mg"), sem("s_merged")
        s_wo, s_sqh, s_ug, s_ssy = sem("s_wo"), sem("s_sqh"), sem("s_ug"), sem("s_ssy")
        s_x1, s_ssx1, s_h2 = sem("s_x1"), sem("s_ssx1"), sem("s_h2")
        s_spill, s_h2p, s_h2T, s_lg, s_ngm, s_ex = (sem("s_spill"), sem("s_h2p"), sem("s_h2T"), sem("s_lg"),
                                                    sem("s_ngm"), sem("s_ex"))
        s_chosen, s_rank, s_tabs, s_gT, s_gTev = (sem("s_chosen"), sem("s_rank"), sem("s_tabs"), sem("s_gT"),
                                                  sem("s_gTev"))
        s_dve = sem("s_dve")
        s_act = sem("s_act")
        s_gup = [[sem(f"s_gup{b}{i}") for i in range(4)] for b in range(2)]
        s_bgu = [sem(f"s_bgu{b}") for b in range(2)]
        s_dlo = [sem(f"s_dlo{b}") for b in range(2)]
        s_dhi = sem("s_dhi")
        s_sel, s_hg, s_hgs, s_turn, s_turned = sem("s_sel"), sem("s_hg"), sem("s_hgs"), sem("s_turn"), sem("s_turned")
        s_half, s_gu, s_glu, s_lin, s_sig = sem("s_half"), sem("s_gu"), sem("s_glu"), sem("s_lin"), sem("s_sig")
        s_tmp, s_actv, s_aT, s_aTev = sem("s_tmp"), sem("s_actv"), sem("s_aT"), sem("s_aTev")
        s_y, s_ysb, s_yrow = sem("s_y"), sem("s_ysb"), sem("s_yrow")
        s_comb, s_fin, s_sqf, s_uf, s_ssf = sem("s_comb"), sem("s_fin"), sem("s_sqf"), sem("s_uf"), sem("s_ssf")
        s_x1b, s_bdb, s_yo, s_out = sem("s_x1b"), sem("s_bdb"), sem("s_yo"), sem("s_out")

        ada_v = w_ada[0].rearrange("(k p) n -> p k n", p=P)
        in_v = w_in[0].rearrange("(k p) n -> p k n", p=P)
        gate_v = w_gate[0].rearrange("(k p) n -> p k n", p=P)
        ba_v = w_branch_a[0].rearrange("(k p) n -> p k n", p=P)
        bb_v = w_branch_b[0].rearrange("(k p) n -> p k n", p=P)
        wo_v = w_out[0].rearrange("(k p) n -> p k n", p=P)
        gu_v = w_gate_up[0].rearrange("e (k p) n -> e p k n", p=P)
        dn_v = w_down[0].rearrange("e (k p) n -> e p k n", p=P)
        bgu_v = b_gate_up[0].rearrange("e (s j h f) -> e j h s f", s=2, j=CT, h=2)
        x_v = x[0].rearrange("(t p) d -> p t d", p=P)
        out_v = out[0].rearrange("(t p) d -> p t d", p=P)

        def page_src(n):
            _, name, i, half = PAGES[n]
            if name == "ada":
                return ada_v[:, 4 * half:4 * half + 4, i * D:(i + 1) * D]
            if name == "gate":
                return gate_v[:, :, i * 512:(i + 1) * 512]
            if name == "wo":
                return wo_v[:, 4 * i:4 * i + 4, :]
            if name in ("ba", "bb"):
                return {"ba": ba_v, "bb": bb_v}[name]
            return in_v[:, :, IN_COL[name]:IN_COL[name] + AW]

        def page_k(n, k):
            cols = D if PAGES[n][1] in ("ada", "wo", "ba", "bb") else AW
            return page(n % RING)[:, k * cols:(k + 1) * cols]

        def page_landed(eng, n):
            eng.wait_ge(s_page[n % RING], 16 * (n // RING + 1))

        def page_free(eng, n):
            signal, count = consumed(n)
            eng.wait_ge({"dve_page": s_dve_page, "branch": s_br, "wo": s_wo, "proj": s_proj}[signal], count)

        block = ctx.enter_context(nc.Block())

        @block.sync
        def _(sp):
            def small_loads(n):
                if n == 0:
                    sp.dma_start(cb_rows[0:KD, :], c.rearrange("a (k p) -> (a k) p", p=P)).then_inc(s_c, 16)
                    sp.dma_start(cb_rows[KD:3 * KD, :], b_gate.rearrange("a (k p) -> (a k) p", p=P)).then_inc(s_c, 16)
                    sp.dma_start(bm, b_ada.rearrange("a (n d) -> (a n) d", d=D)).then_inc(s_bm, 16)
                if n == 2:
                    sp.dma_start(x_sb, x_v).then_inc(s_x, 16)
                if n == 3:
                    sp.dma_start(scale, g_pre_mix[0:1, :].to_broadcast([P, D])).then_inc(s_gain[0], 16)
                if n == 5:
                    sp.dma_start(ws, w_spatial[0].rearrange("g t s -> t g s")).then_inc(s_ws, 16)
                    sp.dma_start(brow[:, P - 1:BW], rel_rev[0]).then_inc(s_brow, 16)
                    sp.dma_start(gain1, g_post_mix[0:1, :].to_broadcast([P, D])).then_inc(s_gain[1], 16)
                if n == 7:
                    sp.dma_start(gain2[:], g_post_ffn[0:1, :].to_broadcast([P, D])).then_inc(s_gain[3], 16)
                    sp.dma_start(ln_g, sgu_ln_g[0:1, :].to_broadcast([P, AW])).then_inc(s_ln, 16)
                    sp.dma_start(ln_b, sgu_ln_b[0:1, :].to_broadcast([P, AW])).then_inc(s_ln, 16)
                    sp.dma_start(wr, w_router[0].rearrange("(k p) e -> p k e", p=P)).then_inc(s_wr, 16)
                    sp.dma_start(b_rt, b_router[0:1, :].to_broadcast([P, NEXP])).then_inc(s_wr, 16)
                    for r in range(2):
                        sp.dma_start(bsb[HD * r:HD * r + HD, :, :],
                                     bs_v[r:r + 1].to_broadcast([HD, KA, P])).then_inc(s_bs, 16)

            bs_v = b_spatial[0].rearrange("(m r) t -> r m t", r=2)
            for n in range(len(PAGES)):
                small_loads(n)
                if n >= RING:
                    page_free(sp, n - RING)
                src = page_src(n)
                sp.dma_start(page(n % RING).rearrange("p (k n) -> p k n", k=src.shape[1]),
                             src).then_inc(s_page[n % RING], 16)

            def load_bgu(slot, e):
                sp.dma_start(bgu[:, slot, :].rearrange("j (h s f) -> j h s f", h=2, s=2),
                             bgu_v[e]).then_inc(s_bgu[slot], 16)

            def load_gu(slot, e, i):
                sp.dma_start(gu_w[slot][:, 2 * i:2 * i + 2, :, :].rearrange("p k s f -> p k (s f)"),
                             gu_v[e, :, 2 * i:2 * i + 2, :]).then_inc(s_gup[slot][i], 16)

            def load_dlo(slot, e):
                sp.dma_start(dlo_w[slot], dn_v[e, :, 0:4, :]).then_inc(s_dlo[slot], 16)

            def load_dhi(e):
                sp.dma_start(dhi_w, dn_v[e, :, 4:8, :]).then_inc(s_dhi, 16)

            load_bgu(0, 0)
            load_bgu(1, 1)
            for i in range(4):
                page_free(sp, len(PAGES) - RING + i)
                load_gu(0, 0, i)
            sp.wait_ge(s_spill, 16 * TT)
            sp.wait_ge(s_lg, TT)
            load_dlo(0, 0)
            load_dhi(0)
            for i in range(4):
                load_gu(1, 1, i)
            load_dlo(1, 1)
            sp.wait_ge(s_tabs, 1)
            done = sp.alloc_register("sp_blocks")
            sp.reg_mov(done, 0)

            def count_blocks(e):
                nb = sp.value_load(nblk_i[0:1, bass.ds(e, 1)], min_val=1, max_val=NBLK)
                sp.reg_add(done, done, nb)
                return sp.snap(done, min_val=1, max_val=NEXP * NBLK)

            total = count_blocks(0)
            sp.wait_ge(s_y, total)
            load_dhi(1)
            with sp.Fori(0, NEXP // 2 - 1) as i:
                for slot in range(2):
                    e = i * 2 + (2 + slot)
                    total = sp.snap(done, min_val=1, max_val=NEXP * NBLK)
                    sp.wait_ge(s_gu, total * 2)
                    load_bgu(slot, e)
                    for q in range(4):
                        load_gu(slot, e, q)
                    sp.wait_ge(s_y, total)
                    load_dlo(slot, e)
                    total = count_blocks(i * 2 + (1 + slot))
                    sp.wait_ge(s_y, total)
                    load_dhi(e)
            sp.dma_start(x1_back, x1_dram[:, :, :]).then_inc(s_x1b, 16)
            sp.dma_start(bd_back, b_down[0]).then_inc(s_bdb, 16)
            for t in range(TT):
                sp.wait_ge(s_yo, t + 1)
                sp.dma_start(out_v[:, t, :], y_out[:, t, :]).then_inc(s_out, 16)
            sp.wait_ge(s_out, 16 * TT)

        @block.gpsimd
        def _(pool):
            g = nc.gpsimd
            g.memset(ident[:], 0.0).then_inc(s_pool, 1)
            g.memset(ones[:], 1.0).then_inc(s_pool, 1)
            g.memset(pick[:], 0.0).then_inc(s_pool, 1)
            g.memset(eps_col, EPS).then_inc(s_pool, 1)
            pool.wait_ge(s_pool, 4)
            g.affine_select(out=ident[:], in_=ident[:], compare_op=ALU.not_equal, fill=1.0, base=0,
                            pattern=[[-1, P]], channel_multiplier=1).then_inc(s_const, 1)
            g.affine_select(out=before, in_=ones[:], compare_op=ALU.is_gt, fill=0.0, base=0,
                            pattern=[[1, P]], channel_multiplier=-1).then_inc(s_const, 1)
            g.affine_select(out=pick[:], in_=pick[:], compare_op=ALU.not_equal, fill=1.0, base=0,
                            pattern=[[-1, CT], [0, TB]], channel_multiplier=1).then_inc(s_const, 1)
            g.iota(iota[:], pattern=[[1, TB]], base=0, channel_multiplier=0,
                   allow_small_or_imprecise_dtypes=True).then_inc(s_const, 1)
            pool.wait_ge(s_brow, 16)
            g.tensor_copy(brow[:, 0:P - 1], brow[:, P - 1:P].to_broadcast([HEADS, P - 1])).then_inc(s_bfill, 1)
            pool.wait_ge(s_bfill, 1)
            pool.dma_start(bias_rows[:, :, :],
                           brow.rearrange("h (a m) -> h a m", a=1).to_broadcast([HEADS, P, BW])).then_inc(s_brows, 16)
            pool.wait_ge(s_h, TT)
            pool.dma_start(scale, g_pre_ffn[0:1, :].to_broadcast([P, D])).then_inc(s_gain[2], 16)
            pool.wait_ge(s_brows, 16)
            window = bass.AP(bias_rows, P - 1, [[BW - 1, P], [P * BW, HEADS], [1, TOK]])
            pool.dma_start(bias, window).then_inc(s_bias, 16)
            pool.wait_ge(s_projev, 8)
            g.affine_select(out=wsT, in_=wsT, compare_op=ALU.is_ge, fill=0.0, base=0,
                            pattern=[[0, GROUPS], [1, P]], channel_multiplier=-1).then_inc(s_wsm, 1)
            pool.wait_ge(s_bias, 16)
            g.memset(bias[0:HD, :, TOK - HD:TOK], NEG).then_inc(s_bmask, 1)
            for t in range(TT):
                pool.wait_ge(s_lnn, t + 1)
                pool.wait_ge(s_ln, 32)
                g.tensor_tensor(vv[:, t, :], vv[:, t, :], ln_g, ALU.mult).then_inc(s_lng, 1)
                pool.wait_ge(s_lng, t + 1)
                g.tensor_tensor(vv[:, t, :], vv[:, t, :], ln_b, ALU.add).then_inc(s_lnd, 1)
            for m in range(KD):
                pool.wait_ge(s_mg, m + 1)
                g.tensor_tensor(mergedT[:, m, :], gates[:, m, :], gates[:, KD + m, :],
                                ALU.add).then_inc(s_merged, 1)
            for t in range(TT):
                pool.wait_ge(s_x1, t + 1)
                pool.dma_start(x1_dram[:, t, :], x_sb[:, t, :]).then_inc(s_spill, 16)
            pool.wait_ge(s_spill, 16 * TT)

        @block.scalar
        def _(act):
            a = nc.scalar
            act.wait_ge(s_cact, 1)
            a.activation(c_sig, c_col, ACT.Sigmoid).then_inc(s_csig, 1)
            act.wait_ge(s_x, 16)
            for t in range(TT):
                a.activation(squares, x_sb[:, t, :], ACT.Square, accum_out=ssq[:, t:t + 1]).then_inc(s_act, 1)
                act.wait_ge(s_act, t + 1)
            act.wait_ge(s_pool, 4)
            a.activation(rms[:, 0:2], ssq[:, 0:2], ACT.Sqrt, scale=1.0 / D, bias=eps_col).then_inc(s_ssx, 1)
            act.wait_ge(s_adasum, 1)
            a.copy(shift, po[:, 2:4, :].rearrange("p b n -> p (b n)")).then_inc(s_mod_a, 1)

            bank = 0

            def evac(dst, func, n_banks=1, **kw):
                nonlocal bank
                act.wait_ge(s_proj, bank + 1)
                a.activation(dst, pp[:, bank % 4, :], func, **kw).then_inc(s_projev, 1)
                bank += 1

            def heads(buf, b):
                return buf[:, 2 * b:2 * b + 2, :].rearrange("p m t -> p (m t)")

            for t in range(TT):
                for q in range(2):
                    act.wait_ge(s_proj, bank + 1)
                    a.copy(hT[:, 4 * q:4 * q + 4, t * P:(t + 1) * P],
                           pp[:, bank % 4, :].rearrange("p (k t) -> p k t", k=4)).then_inc(s_projev, 1)
                    bank += 1
            for b in range(2):
                evac(heads(qT, b), ACT.Copy, scale=float(HD) ** -0.5)
            for b in range(2):
                evac(wsT[:, 4 * b:4 * b + 4, :].rearrange("p g t -> p (g t)"), ACT.Copy)
            for b in range(2):
                evac(heads(kT, b), ACT.Copy)
            act.wait_ge(s_adasum, 4)
            act.wait_ge(s_h, TT)
            a.copy(shift, po[:, 0:2, :].rearrange("p b n -> p (b n)")).then_inc(s_mod_a, 1)
            for t in range(TT):
                evac(v_sb[:, t, :], ACT.Copy)
            for t in range(TT):
                evac(vv[:, t, :], ACT.Gelu)
            for b in range(2):
                evac(heads(ybT, b), ACT.Gelu)
            act.wait_ge(s_mv, TT)
            a.activation(rms[:, 2:4], meanvar[:, :, 1], ACT.Sqrt, bias=eps_col).then_inc(s_lnsq, 1)

            def softmax_exp(h):
                act.wait_ge(s_soft, h + 1)
                a.activation(prob[:, h % 2, 0:P], prob[:, h % 2, 0:P], ACT.Exp, bias=nmax[:, h % 2, 0:1],
                             accum_out=psm[:, h % 2, 0:1])
                a.activation(prob[:, h % 2, P:BW], prob[:, h % 2, P:BW], ACT.Exp, bias=nmax[:, h % 2, 1:2],
                             accum_out=psm[:, h % 2, 1:2]).then_inc(s_exp, 1)

            softmax_exp(0)
            for h in range(HEADS):
                for i in range(2):
                    m = 2 * h + i
                    if i == 0:
                        act.wait_ge(s_proj, bank + 1)
                    ins = a.activation(gates[:, m, :], pp[:, bank % 4, i * TOK:(i + 1) * TOK], ACT.Sigmoid,
                                       bias=bg_col[:, m:m + 1])
                ins.then_inc(s_projev, 1)
                bank += 1
                act.wait_ge(s_pT, h + 1)
                a.copy(probT, po[:, 2, 0:BW]).then_inc(s_pTev, 1)
                if h + 1 < HEADS:
                    softmax_exp(h + 1)

            a.preload_act_table(ACT.Sqrt)
            for t in range(TT):
                act.wait_ge(s_wo, t + 1)
                a.activation(squares[:, 0:512], po[:, 2 * t, :], ACT.Square,
                             accum_out=ssq[:, 2 + 2 * t:3 + 2 * t]).then_inc(s_sqh, 1)
                act.wait_ge(s_ug, 2 * t + 1)
                act.wait_ge(s_sqh, 2 * t + 1)
                a.activation(squares[:, 512:D], po[:, 2 * t + 1, :], ACT.Square,
                             accum_out=ssq[:, 3 + 2 * t:4 + 2 * t]).then_inc(s_sqh, 1)
                a.activation(part_ms[:, t:t + 1], ssq[:, 2 + 2 * t:3 + 2 * t], ACT.Identity, scale=1.0 / D,
                             bias=eps_col).then_inc(s_act, 1)
                act.wait_ge(s_sqh, 2 * t + 2)
                act.wait_ge(s_act, TT + 2 * t + 1)
                a.activation(rms[:, 4 + t:5 + t], ssq[:, 3 + 2 * t:4 + 2 * t], ACT.Sqrt, scale=1.0 / D,
                             bias=part_ms[:, t:t + 1]).then_inc(s_ssy, 1)
                act.wait_ge(s_x1, t + 1)
                a.activation(squares, x_sb[:, t, :], ACT.Square, accum_out=ssq[:, 6 + t:7 + t]).then_inc(s_act, 1)
                act.wait_ge(s_act, TT + 2 * t + 2)
                a.activation(rms[:, 6 + t:7 + t], ssq[:, 6 + t:7 + t], ACT.Sqrt, scale=1.0 / D,
                             bias=eps_col).then_inc(s_ssx1, 1)
                if t == TT - 1:
                    a.preload_act_table(ACT.Exp)
                for q in range(2):
                    act.wait_ge(s_h2p, 2 * t + q + 1)
                    a.copy(h2T[:, 4 * q:4 * q + 4, t * P:(t + 1) * P],
                           pp[:, q, :].rearrange("p (k t) -> p k t", k=4)).then_inc(s_h2T, 1)
            act.wait_ge(s_ngm, 1)
            for t in range(TT):
                ins = a.activation(expo[:, t, :], logit[:, t, :], ACT.Exp, bias=r1[:, t:t + 1])
            ins.then_inc(s_ex, 1)
            a.preload_act_table(ACT.Sigmoid)

            item = act.alloc_register("act_item")
            act.reg_mov(item, 0)
            first_half = act.alloc_register("act_first_half")
            act.reg_mov(first_half, 1)
            act.wait_ge(s_tabs, 1)
            with act.Fori(0, NEXP) as e:
                nb = act.value_load(nblk_i[0:1, bass.ds(e, 1)], min_val=1, max_val=NBLK)
                with act.Fori(0, nb) as b:
                    act.reg_add(item, item, 1)
                    it = act.snap(item, min_val=1, max_val=NEXP * NBLK)
                    halves = (act.snap(first_half, min_val=1, max_val=2 * NEXP * NBLK), it * 2)
                    act.wait_ge(s_turn, it + 1)
                    a.copy(turned, pp[:, TURN, :]).then_inc(s_turned, 1)
                    for hh in range(2):
                        act.wait_ge(s_glu, halves[hh])
                        a.activation(sig[:, hh, :], glu[:, hh, :], ACT.Sigmoid, scale=ALPHA).then_inc(s_sig, 1)
                    for hh in range(2):
                        act.wait_ge(s_aT, halves[hh])
                        a.copy(actT[:, hh, :], pp[:, (TOKS, TURN)[hh], 0:P]).then_inc(s_aTev, 1)
                    act.wait_ge(s_y, it)
                    a.copy(y_sb, pp[:, UP[0], 0:QF]).then_inc(s_ysb, 1)
                    act.reg_add(first_half, first_half, 2)

            a.preload_act_table(ACT.Sqrt)
            act.wait_ge(s_gT, 1)
            a.copy(gateT.rearrange("p t n -> p (t n)"), pp[0:NEXP, TOKS, 0:TOK]).then_inc(s_gTev, 1)
            for t in range(TT):
                act.wait_ge(s_fin, t + 1)
                a.activation(h_sb[:, t, 0:512], po[:, 2 * t, :], ACT.Square,
                             accum_out=ssq[:, 8 + 2 * t:9 + 2 * t]).then_inc(s_sqf, 1)
                act.wait_ge(s_uf, 2 * t + 1)
                a.activation(h_sb[:, t, 512:D], po[:, 2 * t + 1, :], ACT.Square,
                             accum_out=ssq[:, 9 + 2 * t:10 + 2 * t]).then_inc(s_sqf, 1)
                act.wait_ge(s_sqf, 2 * t + 1)
                a.activation(part_ms[:, 2 + t:3 + t], ssq[:, 8 + 2 * t:9 + 2 * t], ACT.Identity, scale=1.0 / D,
                             bias=eps_col).then_inc(s_act, 1)
                act.wait_ge(s_sqf, 2 * t + 2)
                act.wait_ge(s_act, 3 * TT + t + 1)
                a.activation(rms[:, t:t + 1], ssq[:, 9 + 2 * t:10 + 2 * t], ACT.Sqrt, scale=1.0 / D,
                             bias=part_ms[:, 2 + t:3 + t]).then_inc(s_ssf, 1)

        @block.vector
        def _(dve):
            v = nc.vector
            chain = 0

            def link(ins):
                nonlocal chain
                chain += 1
                ins.then_inc(s_dve, 1)
                dve.wait_ge(s_dve, chain)

            dve.wait_ge(s_cT, 1)
            v.tensor_copy(cb_col, pp[:, 0, 0:3 * KD]).then_inc(s_cact, 1)
            dve.wait_ge(s_csig, 1)
            v.tensor_tensor(c_act, c_col, c_sig, ALU.mult).then_inc(s_cact, 1)
            dve.wait_ge(s_cact, 2)
            dve.wait_ge(s_bm, 16)

            def modulation(n):
                if n >= 2:
                    dve.wait_ge(s_adasum, n - 1)
                for half in range(2):
                    pg = page_of("ada", n, half)
                    page_landed(dve, pg)
                    for k in range(4):
                        kk = 4 * half + k
                        if kk == 0:
                            link(v.tensor_scalar(acc[:, n % 2, :], page_k(pg, k), c_act[:, kk:kk + 1], None, ALU.mult))
                            link(v.scalar_tensor_tensor(out=acc[0:NMOD, n % 2, :], in0=bm, scalar=ident[0:NMOD, n:n + 1],
                                                        in1=acc[0:NMOD, n % 2, :], op0=ALU.mult, op1=ALU.add))
                            continue
                        ins = v.scalar_tensor_tensor(out=acc[:, n % 2, :], in0=page_k(pg, k), scalar=c_act[:, kk:kk + 1],
                                                     in1=acc[:, n % 2, :], op0=ALU.mult, op1=ALU.add)
                        if k < 3:
                            link(ins)
                        else:
                            ins.then_inc(s_dve_page, 1)
                            dve.wait_ge(s_dve_page, 2 * n + half + 1)

            def mod_bank(n):
                return po[:, 2:4, :] if n % 2 == 0 else po[:, 0:2, :]

            def flat2(ap):
                return ap.rearrange("p b n -> p (b n)")

            modulation(0)
            modulation(1)
            dve.wait_ge(s_ssx, 1)
            link(v.reciprocal(rstd[:, 0:2], rms[:, 0:2]))
            dve.wait_ge(s_adasum, 2)
            dve.wait_ge(s_gain[0], 16)
            v.scalar_tensor_tensor(out=scale, in0=flat2(mod_bank(1)), scalar=1.0, in1=scale,
                                   op0=ALU.add, op1=ALU.mult).then_inc(s_scale, 1)
            dve.wait_ge(s_scale, 1)
            dve.wait_ge(s_mod_a, 1)
            for t in range(TT):
                link(v.scalar_tensor_tensor(out=h_sb[:, t, :], in0=x_sb[:, t, :], scalar=rstd[:, t:t + 1], in1=scale,
                                            op0=ALU.mult, op1=ALU.mult))
                v.tensor_tensor(h_sb[:, t, :], h_sb[:, t, :], shift, ALU.add).then_inc(s_h, 1)
            modulation(2)
            dve.wait_ge(s_adasum, 3)
            dve.wait_ge(s_gain[1], 16)
            v.tensor_tensor(gain1, gain1, flat2(mod_bank(2)), ALU.mult).then_inc(s_mod_v, 1)
            modulation(3)
            modulation(4)
            dve.wait_ge(s_adasum, 5)
            dve.wait_ge(s_gain[2], 16)
            v.scalar_tensor_tensor(out=scale, in0=flat2(mod_bank(4)), scalar=1.0, in1=scale,
                                   op0=ALU.add, op1=ALU.mult).then_inc(s_mod_v, 1)
            modulation(5)
            dve.wait_ge(s_adasum, 6)
            dve.wait_ge(s_gain[3], 16)
            v.tensor_tensor(gain2[:], gain2[:], flat2(mod_bank(5)), ALU.mult).then_inc(s_mod_v, 1)

            dve.wait_ge(s_projev, 14)
            for t in range(TT):
                link(v.bn_stats(stats[:, t, :], vv[:, t, :]))
                v.bn_aggr(meanvar[:, t, :], stats[:, t, :]).then_inc(s_mv, 1)
            dve.wait_ge(s_lnsq, 1)
            link(v.reciprocal(rstd[:, 2:4], rms[:, 2:4]))
            for t in range(TT):
                v.tensor_scalar(vv[:, t, :], vv[:, t, :], meanvar[:, t, 0:1], rstd[:, 2 + t:3 + t],
                                ALU.subtract, ALU.mult).then_inc(s_lnn, 1)
            def scores_bias(h):
                dve.wait_ge(s_bmask, 1)
                dve.wait_ge(s_score, h + 1)
                if h >= 2:
                    dve.wait_ge(s_pT, h - 1)
                v.tensor_tensor(prob[:, h % 2, 0:P], po[:, h % 2, 0:P], bias[:, h, P:TOK], ALU.add)
                link(v.tensor_tensor(prob[:, h % 2, P:BW], po[:, h % 2, P:BW], bias[:, h, :], ALU.add))
                v.tensor_reduce(nmax[:, h % 2, 0:1], prob[:, h % 2, 0:P], AX.X, ALU.max, negate=True)
                v.tensor_reduce(nmax[:, h % 2, 1:2], prob[:, h % 2, P:BW], AX.X, ALU.max,
                                negate=True).then_inc(s_soft, 1)

            def normalise(h):
                dve.wait_ge(s_exp, h + 1)
                link(v.reciprocal(prc[:, h % 2, :], psm[:, h % 2, :]))
                v.tensor_scalar(prob[:, h % 2, 0:P], prob[:, h % 2, 0:P], prc[:, h % 2, 0:1], None, ALU.mult)
                v.tensor_scalar(prob[:, h % 2, P:BW], prob[:, h % 2, P:BW], prc[:, h % 2, 1:2], None,
                                ALU.mult).then_inc(s_prob, 1)

            def heads_out(m):
                dve.wait_ge(s_pv, 2 * m + 2)
                v.tensor_copy(yaT[:, m, :], po[:, 3, 0:TOK]).then_inc(s_ya, 1)

            scores_bias(0)
            dve.wait_ge(s_bs, 32)
            dve.wait_ge(s_projev, 16)
            for m in range(KA):
                dve.wait_ge(s_sgu, m // 2 + 1)
                src = po[:, 2 + m // 2, (m % 2) * TOK:(m % 2 + 1) * TOK].rearrange("p (b t) -> p b t", b=TT)
                dst = prob[:, 1, 0:TOK]
                link(v.tensor_tensor(dst.rearrange("p (b t) -> p b t", b=TT), src,
                                     bsb[:, m:m + 1, :].to_broadcast([P, TT, P]), ALU.add))
                v.tensor_tensor(ybT[:, m, :], ybT[:, m, :], dst, ALU.mult).then_inc(s_yb, 1)
                dve.wait_ge(s_yb, m + 1)
            for h in range(HEADS):
                if h >= 2 and h % 2 == 0:
                    heads_out(h // 2 - 1)
                if h + 1 < HEADS:
                    scores_bias(h + 1)
                normalise(h)
            heads_out(KA - 1)
            v.memset(y_sb, 0.0).then_inc(s_ysb, 1)
            v.memset(selgT, 0.0).then_inc(s_ysb, 1)

            for m in range(KD):
                dve.wait_ge(s_br, m + 1)
                v.tensor_tensor(gates[:, m, :], pp[:, m % 4, 0:TOK], gates[:, m, :], ALU.mult)
                v.tensor_tensor(gates[:, KD + m, :], pp[:, m % 4, TOK:2 * TOK], gates[:, KD + m, :],
                                ALU.mult).then_inc(s_mg, 1)

            dve.wait_ge(s_mod_a, 2)
            for t in range(TT):
                dve.wait_ge(s_wo, t + 1)
                v.tensor_tensor(h_sb[:, t, 512:D], po[:, 2 * t + 1, :], gain1[:, 512:D], ALU.mult).then_inc(s_ug, 1)
                dve.wait_ge(s_sqh, 2 * t + 1)
                v.tensor_tensor(h_sb[:, t, 0:512], po[:, 2 * t, :], gain1[:, 0:512], ALU.mult).then_inc(s_ug, 1)
                dve.wait_ge(s_ug, 2 * t + 2)
                dve.wait_ge(s_ssy, t + 1)
                link(v.reciprocal(rstd[:, 4 + t:5 + t], rms[:, 4 + t:5 + t]))
                v.scalar_tensor_tensor(out=x_sb[:, t, :], in0=h_sb[:, t, :], scalar=rstd[:, 4 + t:5 + t],
                                       in1=x_sb[:, t, :], op0=ALU.mult, op1=ALU.add).then_inc(s_x1, 1)
                dve.wait_ge(s_x1, t + 1)
                link(v.tensor_tensor(h_sb[:, t, :], x_sb[:, t, :], scale, ALU.mult))
                dve.wait_ge(s_ssx1, t + 1)
                link(v.reciprocal(rstd[:, 6 + t:7 + t], rms[:, 6 + t:7 + t]))
                v.scalar_tensor_tensor(out=h_sb[:, t, :], in0=h_sb[:, t, :], scalar=rstd[:, 6 + t:7 + t],
                                       in1=shift, op0=ALU.mult, op1=ALU.add).then_inc(s_h2, 1)

            dve.wait_ge(s_wr, 32)
            for t in range(TT):
                dve.wait_ge(s_lg, t + 1)
                link(v.tensor_tensor(logit[:, t, :], pp[:, 2 + t, 0:NEXP], b_rt, ALU.add))
                link(v.max(top8[:, t, :], logit[:, t, :]))
            v.tensor_scalar(r1[:, 0:2], top8[:, :, 0], -1.0, None, ALU.mult).then_inc(s_ngm, 1)
            for t in range(TT):
                fourth = top8[:, t, TOPK - 1:TOPK]
                v.tensor_scalar(above[:, t, :], logit[:, t, :], fourth, None, ALU.is_gt)
                link(v.tensor_scalar(equal[:, t, :], logit[:, t, :], fourth, None, ALU.is_equal))
            link(v.tensor_reduce(r1[:, 2:4], above, AX.X, ALU.add))
            link(v.tensor_scalar(r1[:, 2:4], r1[:, 2:4], -1.0, float(TOPK), ALU.mult, ALU.add))
            for t in range(TT):
                link(v.tensor_tensor_scan(upto[:, t, :], ones[:, 0:NEXP], equal[:, t, :], 0.0, ALU.mult, ALU.add))
                link(v.scalar_tensor_tensor(out=equal[:, t, :], in0=upto[:, t, :], scalar=r1[:, 2 + t:3 + t],
                                            in1=equal[:, t, :], op0=ALU.is_le, op1=ALU.mult))
            v.tensor_tensor(chosen, above, equal, ALU.add).then_inc(s_chosen, 1)
            dve.wait_ge(s_chosen, 1)
            dve.wait_ge(s_ex, 1)
            link(v.tensor_tensor(expo, expo, chosen, ALU.mult))
            link(v.tensor_reduce(r1[:, 4:6], expo, AX.X, ALU.add))
            link(v.reciprocal(r1[:, 6:8], r1[:, 4:6]))
            for t in range(TT):
                ins = v.tensor_scalar(gate_tab[:, t, :], expo[:, t, :], r1[:, 6 + t:7 + t], None, ALU.mult)
            link(ins)
            dve.wait_ge(s_rank, 1)
            counts = pp[:, 0, 2 * NEXP:3 * NEXP]
            link(v.tensor_copy(nblk_f, counts))
            for m in range(7):
                ins = v.tensor_scalar(cmp7[:, :, m], nblk_f, float(TB * (m + 1)), None, ALU.is_gt)
            link(ins)
            link(v.tensor_reduce(nblk_f, cmp7, AX.X, ALU.add))
            v.tensor_scalar(nblk_i[:], nblk_f, 1.0, None, ALU.add)
            link(v.scalar_tensor_tensor(out=rank, in0=pp[:, 0, 0:2 * NEXP].rearrange("p (t e) -> p t e", t=TT),
                                        scalar=1.0, in1=chosen, op0=ALU.add, op1=ALU.mult))
            for b in range(NBLK):
                ins = v.tensor_scalar(rank_tab[:, :, b, :], rank, -1.0 - TB * b, None, ALU.add)
            ins.then_inc(s_tabs, 1)
            dve.wait_ge(s_tabs, 1)
            dve.wait_ge(s_const, 4)

            item = dve.alloc_register("dve_item")
            dve.reg_mov(item, 0)
            first_half = dve.alloc_register("dve_first_half")
            dve.reg_mov(first_half, 1)
            with dve.Fori(0, NEXP) as e:
                nb = dve.value_load(nblk_i[0:1, bass.ds(e, 1)], min_val=1, max_val=NBLK)
                with dve.Fori(0, nb) as b:
                    dve.reg_add(item, item, 1)
                    it = dve.snap(item, min_val=1, max_val=NEXP * NBLK)
                    halves = (dve.snap(first_half, min_val=1, max_val=2 * NEXP * NBLK), it * 2)
                    dve.wait_ge(s_turn, it)
                    for t in range(TT):
                        rk = rank_tab[:, t, bass.ds(b, 1), bass.ds(e, 1)]
                        gt = gate_tab[:, t, bass.ds(e, 1)]
                        v.tensor_scalar(sel[:, t, :], iota[:], rk, None, ALU.is_equal)
                        ins = v.tensor_scalar(selg[:, t, :, :],
                                              iota[:].rearrange("p (a j) -> p a j", a=1).to_broadcast([P, CT, TB]),
                                              rk, gt, ALU.is_equal, ALU.mult)
                    ins.then_inc(s_sel, 1)
                    dve.wait_ge(s_hg, it)
                    v.tensor_copy(hg.rearrange("p h n -> p (h n)"), pp[:, TOKS, 0:QF]).then_inc(s_hgs, 1)
                    for hh in range(2):
                        n = halves[hh]
                        up = pp[:, UP[hh], :]
                        dve.wait_ge(s_gu, n)
                        v.tensor_scalar(glu[:, hh, :], up[:, 0:QH], LIMIT, None, ALU.min).then_inc(s_glu, 1)
                        v.tensor_scalar(lin[:, hh, :], up[:, QH:QF], LIMIT, -LIMIT, ALU.min, ALU.max).then_inc(s_lin, 1)
                        dve.wait_ge(s_lin, n)
                        v.scalar_tensor_tensor(out=lin[:, hh, :], in0=lin[:, hh, :], scalar=1.0, in1=glu[:, hh, :],
                                               op0=ALU.add, op1=ALU.mult).then_inc(s_tmp, 1)
                        dve.wait_ge(s_tmp, n)
                        dve.wait_ge(s_sig, n)
                        v.tensor_tensor(act_sb[:, hh, :], lin[:, hh, :], sig[:, hh, :], ALU.mult).then_inc(s_actv, 1)
                    dve.reg_add(first_half, first_half, 2)

            dve.wait_ge(s_x1b, 16)
            for t in range(TT):
                dve.wait_ge(s_fin, t + 1)
                v.tensor_tensor(y_out[:, t, 512:D], po[:, 2 * t + 1, :], gain2[:, 512:D], ALU.mult).then_inc(s_uf, 1)
                dve.wait_ge(s_sqf, 2 * t + 1)
                v.tensor_tensor(y_out[:, t, 0:512], po[:, 2 * t, :], gain2[:, 0:512], ALU.mult).then_inc(s_uf, 1)
                dve.wait_ge(s_uf, 2 * t + 2)
                dve.wait_ge(s_ssf, t + 1)
                link(v.reciprocal(rstd[:, t:t + 1], rms[:, t:t + 1]))
                v.scalar_tensor_tensor(out=y_out[:, t, :], in0=y_out[:, t, :], scalar=rstd[:, t:t + 1],
                                       in1=x1_back[:, t, :], op0=ALU.mult, op1=ALU.add).then_inc(s_yo, 1)

        @block.tensor
        def _(pe):
            t_ = nc.tensor
            pe.wait_ge(s_const, 1)
            pe.wait_ge(s_c, 32)
            t_.transpose(pp[:, 0, 0:3 * KD], cb_rows, ident[0:3 * KD, 0:3 * KD]).then_inc(s_cT, 1)

            def modulation_sum(n):
                if n == 0:
                    pe.wait_ge(s_pool, 2)
                elif n == 2:
                    pe.wait_ge(s_mod_a, 1)
                elif n == 3:
                    pe.wait_ge(s_scale, 1)
                elif n == 4:
                    pe.wait_ge(s_mod_v, 1)
                elif n == 5:
                    pe.wait_ge(s_mod_a, 2)
                pe.wait_ge(s_dve_page, 2 * n + 2)
                for half in range(2):
                    mm = t_.matmul(po[:, 2 * (1 - n % 2) + half, :], ones[:], acc[:, n % 2, half * 512:(half + 1) * 512],
                                   start=True, stop=True)
                mm.then_inc(s_adasum, 1)

            modulation_sum(0)
            modulation_sum(1)

            bank = 0

            def next_bank():
                nonlocal bank
                if bank >= 4:
                    pe.wait_ge(s_projev, bank - 3)
                bank += 1
                return pp[:, (bank - 1) % 4, :]

            for t in range(TT):
                pe.wait_ge(s_h, t + 1)
                for q in range(2):
                    ps = next_bank()
                    for i in range(4):
                        mm = t_.transpose(ps[:, i * P:(i + 1) * P], h_sb[:, t, (4 * q + i) * P:(4 * q + i + 1) * P],
                                          ident[:])
                    mm.then_inc(s_proj, 1)
            pe.wait_ge(s_projev, 4)

            def page_T(name):
                pg = page_of(name)
                page_landed(pe, pg)
                for b in range(2):
                    ps = next_bank()
                    for i in range(2):
                        m = 2 * b + i
                        for k in range(KD):
                            mm = t_.matmul(ps[:, i * TOK:(i + 1) * TOK], page_k(pg, k)[:, m * P:(m + 1) * P],
                                           hT[:, k, :], start=(k == 0), stop=(k == KD - 1))
                    mm.then_inc(s_proj, 1)

            def page_rows(name):
                pg = page_of(name)
                page_landed(pe, pg)
                for t in range(TT):
                    ps = next_bank()
                    for k in range(KD):
                        mm = t_.matmul(ps, hT[:, k, t * P:(t + 1) * P], page_k(pg, k), start=(k == 0),
                                       stop=(k == KD - 1))
                    mm.then_inc(s_proj, 1)

            page_T("q")
            pe.wait_ge(s_ws, 16)
            for b in range(2):
                ps = next_bank()
                for i in range(4):
                    mm = t_.transpose(ps[:, i * P:(i + 1) * P], ws[:, 4 * b + i, :], ident[:])
                mm.then_inc(s_proj, 1)
            modulation_sum(2)
            page_T("k")
            modulation_sum(3)
            page_rows("v")
            modulation_sum(4)
            page_rows("vv")
            modulation_sum(5)
            page_T("u")

            def spatial():
                pe.wait_ge(s_lnd, TT)
                pe.wait_ge(s_wsm, 1)
                pe.wait_ge(s_mod_v, 2)
                for m in range(KA):
                    for r in range(2):
                        for b in range(TT):
                            g = 2 * m + r
                            col = (m % 2) * TOK + b * P
                            mm = t_.matmul(po[HD * r:HD * r + HD, 2 + m // 2, col:col + P],
                                           vv[:, b, g * HD:(g + 1) * HD], wsT[:, g, :], start=True, stop=True)
                    if m % 2:
                        mm.then_inc(s_sgu, 1)

            def scores(h):
                m, r = h // 2, HD * (h % 2)
                if h == 0:
                    pe.wait_ge(s_projev, 10)
                    pe.wait_ge(s_mod_v, 3)
                if h >= 2:
                    pe.wait_ge(s_soft, h - 1)
                t_.matmul(po[:, h % 2, 0:P], qT[r:r + HD, m, 0:P], kT[r:r + HD, m, 0:P], start=True, stop=True)
                t_.matmul(po[:, h % 2, P:BW], qT[r:r + HD, m, P:TOK], kT[r:r + HD, m, :], start=True,
                          stop=True).then_inc(s_score, 1)

            scores(0)
            scores(1)
            for h in range(HEADS):
                pg = page_of("gate", h // 2)
                if h % 2 == 0:
                    page_landed(pe, pg)
                ps = next_bank()
                for i in range(2):
                    m = 2 * (h % 2) + i
                    for k in range(KD):
                        mm = t_.matmul(ps[:, i * TOK:(i + 1) * TOK], page_k(pg, k)[:, m * P:(m + 1) * P], hT[:, k, :],
                                       start=(k == 0), stop=(k == KD - 1))
                mm.then_inc(s_proj, 1)
                if h == 0:
                    spatial()
                pe.wait_ge(s_prob, h + 1)
                if h == 0:
                    pe.wait_ge(s_yb, KA)
                for i in range(3):
                    mm = t_.transpose(po[:, 2, i * P:(i + 1) * P], prob[:, h % 2, i * P:(i + 1) * P], ident[:])
                mm.then_inc(s_pT, 1)
                if h + 2 < HEADS:
                    scores(h + 2)
                pe.wait_ge(s_pTev, h + 1)
                if h >= 2 and h % 2 == 0:
                    pe.wait_ge(s_ya, h // 2)
                r, col = HD * (h % 2), 0
                t_.matmul(po[r:r + HD, 3, col:col + P], v_sb[:, 0, h * HD:(h + 1) * HD], probT[:, 0:P], start=True,
                          stop=True)
                for b in range(TT):
                    mm = t_.matmul(po[r:r + HD, 3, col + P:col + TOK], v_sb[:, b, h * HD:(h + 1) * HD],
                                   probT[:, (1 + b) * P:(2 + b) * P], start=(b == 0), stop=(b == 1))
                mm.then_inc(s_pv, 1)

            pe.wait_ge(s_ya, KA)
            pe.wait_ge(s_projev, bank)
            pga, pgb = page_of("ba"), page_of("bb")
            page_landed(pe, pga)
            page_landed(pe, pgb)
            for m in range(KD):
                if m >= 4:
                    pe.wait_ge(s_mg, m - 3)
                for half, (pg, src) in enumerate(((pga, yaT), (pgb, ybT))):
                    for k in range(KA):
                        mm = t_.matmul(pp[:, m % 4, half * TOK:(half + 1) * TOK], page_k(pg, k)[:, m * P:(m + 1) * P],
                                       src[:, k, :], start=(k == 0), stop=(k == KA - 1))
                mm.then_inc(s_br, 1)

            for i in range(2):
                page_landed(pe, page_of("wo", i))
            for t in range(TT):
                for k in range(KD):
                    if t == 0:
                        pe.wait_ge(s_merged, k + 1)
                    for half in range(2):
                        mm = t_.matmul(po[:, 2 * t + half, :], mergedT[:, k, t * P:(t + 1) * P],
                                       page_k(page_of("wo", k // 4), k % 4)[:, half * 512:(half + 1) * 512],
                                       start=(k == 0), stop=(k == KD - 1))
                mm.then_inc(s_wo, 1)

            pe.wait_ge(s_wr, 32)
            pe.wait_ge(s_mg, KD)
            for t in range(TT):
                pe.wait_ge(s_h2, t + 1)
                for q in range(2):
                    if t:
                        pe.wait_ge(s_h2T, q + 1)
                    for i in range(4):
                        mm = t_.transpose(pp[:, q, i * P:(i + 1) * P], h_sb[:, t, (4 * q + i) * P:(4 * q + i + 1) * P],
                                          ident[:])
                    mm.then_inc(s_h2p, 1)
                for k in range(KD):
                    if k % 4 == 0:
                        pe.wait_ge(s_h2T, 2 * t + k // 4 + 1)
                    mm = t_.matmul(pp[:, 2 + t, 0:NEXP], h2T[:, k, t * P:(t + 1) * P], wr[:, k, :], start=(k == 0),
                                   stop=(k == KD - 1))
                mm.then_inc(s_lg, 1)

            pe.wait_ge(s_ysb, 2)
            zeros = y_sb.bitcast(BF16)
            for b in range(4):
                mm = t_.matmul(po[:, b, :], zeros[:, 0:P], zeros, start=True, stop=False, skip_group_check=True)
            mm.then_inc(s_turn, 1)
            pe.wait_ge(s_const, 4)
            pe.wait_ge(s_chosen, 1)
            t_.matmul(pp[:, 0, 0:NEXP], before, chosen[:, 0, :], start=True, stop=True)
            for col, second in ((NEXP, before), (2 * NEXP, ones[:])):
                t_.matmul(pp[:, 0, col:col + NEXP], ones[:], chosen[:, 0, :], start=True, stop=False)
                mm = t_.matmul(pp[:, 0, col:col + NEXP], second, chosen[:, 1, :], start=False, stop=True)
            mm.then_inc(s_rank, 1)
            pe.wait_ge(s_tabs, 1)

            def combine(it):
                pe.wait_ge(s_ysb, it + 1)
                for rnd in range(2):
                    for j in range(CT):
                        half = j // 2
                        t = (j + rnd) % 2
                        col = (j % 2) * QF
                        mm = t_.matmul(po[:, 2 * t + half, col:col + QF], selgT[j * TB:(j + 1) * TB, t, :],
                                       y_sb[j * TB:(j + 1) * TB, :], start=False, stop=False, skip_group_check=True)
                    if rnd == 0:
                        mm.then_inc(s_half, 1)
                        pe.wait_ge(s_half, it)
                return mm

            item = pe.alloc_register("pe_item")
            pe.reg_mov(item, 0)
            first_half = pe.alloc_register("pe_first_half")
            pe.reg_mov(first_half, 1)
            with pe.Fori(0, NEXP // 2) as i:
                for slot in range(2):
                    nb = pe.value_load(nblk_i[0:1, bass.ds(i * 2 + slot, 1)], min_val=1, max_val=NBLK)
                    with pe.Fori(0, nb) as b:
                        pe.reg_add(item, item, 1)
                        it = pe.snap(item, min_val=1, max_val=NEXP * NBLK)
                        halves = (pe.snap(first_half, min_val=1, max_val=2 * NEXP * NBLK), it * 2)
                        landed = i * 16 + 16
                        pe.wait_ge(s_sel, it)
                        for t in range(TT):
                            for j in range(CT):
                                mm = t_.matmul(pp[j * TB:(j + 1) * TB, TOKS, 0:QF], sel[:, t, :],
                                               h_sb[:, t, j * QF:(j + 1) * QF], start=(t == 0), stop=(t == TT - 1))
                        mm.then_inc(s_hg, 1)
                        combine(it)
                        pe.wait_ge(s_bgu[slot], landed)
                        for t in range(TT):
                            t_.transpose(pp[:, TURN, 256 + t * P:256 + (t + 1) * P],
                                         selg[:, t, :, :].rearrange("p c j -> p (c j)"), ident[:])
                        pe.wait_ge(s_hgs, it)
                        for hh in range(2):
                            mm = t_.transpose(pp[:, TURN, hh * P:(hh + 1) * P], hg[:, hh, :], ident[:])
                        mm.then_inc(s_turn, 1)
                        for hh in range(2):
                            for j in range(CT):
                                t_.matmul(pp[j * TB:(j + 1) * TB, UP[hh], 0:QF], pick[:, j, :],
                                          bgu[:, slot, hh * QF:(hh + 1) * QF], start=True, stop=False,
                                          skip_group_check=True)
                        pe.wait_ge(s_turned, it)
                        for hh in range(2):
                            for k in range(KD):
                                if hh == 0 and k % 2 == 0:
                                    pe.wait_ge(s_gup[slot][k // 2], landed)
                                for j in range(CT):
                                    col = j * QF + hh * QH
                                    mm = t_.matmul(pp[j * TB:(j + 1) * TB, UP[hh], 0:QF].rearrange("p (s f) -> p s f", s=2),
                                                   hgT[:, k % 2, (k // 2) * TB:(k // 2 + 1) * TB],
                                                   gu_w[slot][:, k, :, col:col + QH], start=False, stop=(k == KD - 1),
                                                   skip_group_check=True)
                            mm.then_inc(s_gu, 1)

                        def turn_half(hh):
                            pe.wait_ge(s_actv, halves[hh])
                            t_.transpose(pp[:, (TOKS, TURN)[hh], 0:P], act_sb[:, hh, :], ident[:]).then_inc(s_aT, 1)

                        turn_half(0)
                        pe.wait_ge(s_dlo[slot], landed)
                        pe.wait_ge(s_aTev, halves[0])
                        for n, cf in enumerate((0, 2, 4, 6, 1, 3, 5, 7)):
                            if cf == 4:
                                pe.wait_ge(s_dhi, i * 32 + 16 * (slot + 1))
                            if cf == 6:
                                turn_half(1)
                            if cf == 1:
                                pe.wait_ge(s_aTev, it * 2)
                            w = dlo_w[slot][:, cf, :] if cf < 4 else dhi_w[:, cf - 4, :]
                            for j in range(CT):
                                mm = t_.matmul(pp[j * TB:(j + 1) * TB, UP[0], 0:QF],
                                               actT[:, cf % 2, (cf // 2) * TB:(cf // 2 + 1) * TB],
                                               w[:, j * QF:(j + 1) * QF], start=(n == 0), stop=(n == KD - 1))
                        mm.then_inc(s_y, 1)
                        pe.reg_add(first_half, first_half, 2)
            for t in range(TT):
                mm = t_.transpose(pp[0:NEXP, TOKS, t * P:(t + 1) * P], gate_tab[:, t, :], ident[:])
            mm.then_inc(s_gT, 1)
            pe.reg_add(item, item, 1)
            combine(pe.snap(item, min_val=1, max_val=NEXP * NBLK + 1)).then_inc(s_comb, 1)
            pe.wait_ge(s_comb, 1)
            pe.wait_ge(s_gTev, 1)
            pe.wait_ge(s_bdb, 16)
            for t in range(TT):
                for half in range(2):
                    mm = t_.matmul(po[:, 2 * t + half, :], gateT[:, t, :], bd_back[:, half * 512:(half + 1) * 512],
                                   start=False, stop=True, skip_group_check=True)
                mm.then_inc(s_fin, 1)


_INS = ["x", "c", "w_ada", "b_ada", "g_pre_mix", "g_post_mix", "w_in", "rel_bias", "sgu_ln_g", "sgu_ln_b",
        "w_spatial", "b_spatial", "w_branch_a", "w_branch_b", "w_gate", "b_gate", "w_out", "g_pre_ffn",
        "g_post_ffn", "w_router", "b_router", "w_gate_up", "b_gate_up", "w_down", "b_down"]
_OUTS = [((1, TOK, D), "float32")]


def kernel(**inputs):
    import numpy as _np
    import concourse.bacc as _bacc
    from concourse import mybir as _mybir
    from concourse.bass_utils import run_bass_kernel_spmd as _run

    nc = _bacc.Bacc("TRN2", target_bir_lowering=False, num_devices=1)
    arrays, args = {}, []
    for name in _INS:
        a = _np.asarray(inputs[name])
        if name == "rel_bias":
            a = a[:, :, ::-1]
        a = _np.ascontiguousarray(a)
        arrays[f"in_{name}_dram"] = a
        args.append(nc.dram_tensor(f"in_{name}_dram", a.shape, _mybir.dt.from_np(a.dtype), kind="ExternalInput").ap())
    for i, (shape, dtype) in enumerate(_OUTS):
        dt = _mybir.dt.from_np(_np.dtype(dtype))
        args.append(nc.dram_tensor(f"out_{i}_dram", shape, dt, kind="ExternalOutput").ap())
    block_program(nc, *args)
    r = _run(nc, [arrays], core_ids=[0])
    return r.results[0]["out_0_dram"]
```

```python
from contextlib import ExitStack

import concourse.bass as bass
from concourse import mybir

ALU = mybir.AluOpType
ACT = mybir.ActivationFunctionType
F32 = mybir.dt.float32
I32 = mybir.dt.int32
BF16 = mybir.dt.bfloat16
AX = mybir.AxisListType

P = 128
TOK, D = 256, 1024
TT = TOK // P
KD = D // P
AW = 512
KA = AW // P
HEADS, HD = 8, 64
NREL = 257
GROUPS = 8
NMOD = 6
NEXP, TOPK = 32, 4
F = 1024
TB = 64
NARROW = 32
NBLK = TOK // TB
BR = 256
NBR = F // BR
LIMIT, ALPHA, EPS = 7.0, 1.702, 1e-6
NEG = -1e30
BW = 3 * P
PAGE = 4096
RING = 5

PAGES = [("dve", "ada", 0, 0), ("dve", "ada", 0, 1), ("dve", "ada", 1, 0), ("dve", "ada", 1, 1)]
PAGES += [("pe", "q", 0, 0)]
for _n, _name in enumerate(("k", "v", "vv", "u")):
    PAGES += [("pe", _name, 0, 0), ("dve", "ada", _n + 2, 0), ("dve", "ada", _n + 2, 1)]
PAGES += [("pe", "gate", _n, 0) for _n in range(4)]
PAGES += [("pe", "ba", 0, 0), ("pe", "bb", 0, 0), ("pe", "wo", 0, 0), ("pe", "wo", 1, 0)]
IN_COL = {"q": 0, "k": AW, "v": 2 * AW, "u": 3 * AW, "vv": 4 * AW}


def page_of(name, part=0, half=0):
    return [n for n, pg in enumerate(PAGES) if pg[1:] == (name, part, half)][0]


def consumed(n):
    who, name, i, _ = PAGES[n]
    if who == "dve":
        return "dve_page", sum(1 for pg in PAGES[:n + 1] if pg[0] == "dve")
    if name in ("ba", "bb"):
        return "branch", KD
    if name == "wo":
        return "wo", TT
    return "proj", 4 + 2 * sum(1 for pg in PAGES[:n + 1] if pg[0] == "pe") + (0 if name == "q" else 2)


def block_program(nc, x, c, w_ada, b_ada, g_pre_mix, g_post_mix, w_in, rel_rev, sgu_ln_g, sgu_ln_b,
                  w_spatial, b_spatial, w_branch_a, w_branch_b, w_gate, b_gate, w_out, g_pre_ffn,
                  g_post_ffn, w_router, b_router, w_gate_up, b_gate_up, w_down, b_down, out):
    with ExitStack() as ctx:
        def sb(name, shape, dt=F32):
            return ctx.enter_context(nc.sbuf_tensor(name, shape, dt))

        def psum(name, shape):
            return ctx.enter_context(nc.psum_tensor(name, shape, F32))

        def sem(name):
            return ctx.enter_context(nc.semaphore(name))

        arena = sb("arena", [P, 11 * PAGE])

        def page(n, cols=PAGE):
            return arena[:, n * PAGE:n * PAGE + cols]

        def part(start, cols):
            return arena[:, start:start + cols]

        at5 = 5 * PAGE
        acc = part(at5, 2 * D).rearrange("p (b d) -> p b d", b=2)
        vv = part(at5 + 2048, TT * AW).rearrange("p (t w) -> p t w", t=TT)
        ws = part(at5 + 3072, GROUPS * P).rearrange("p (g s) -> p g s", g=GROUPS)
        at6 = 6 * PAGE
        qT = part(at6, KA * TOK).rearrange("p (m t) -> p m t", m=KA)
        kT = part(at6 + 1024, KA * TOK).rearrange("p (m t) -> p m t", m=KA)
        v_sb = part(at6 + 2048, TT * AW).rearrange("p (t w) -> p t w", t=TT)
        wsT = part(at6 + 3072, GROUPS * P).rearrange("p (g t) -> p g t", g=GROUPS)
        at7 = 7 * PAGE
        bias = part(at7, HEADS * TOK).rearrange("p (h k) -> p h k", h=HEADS)
        ybT = part(at7 + 2048, KA * TOK).rearrange("p (m t) -> p m t", m=KA)
        bsb = part(at7 + 3072, KA * P).rearrange("p (m t) -> p m t", m=KA)
        at8 = 8 * PAGE
        x_sb = part(at8, TT * D).rearrange("p (t d) -> p t d", t=TT)
        hT = part(at8 + 2048, KD * TOK).rearrange("p (k t) -> p k t", k=KD)
        mergedT = hT
        gates = part(at8 + 4096, 2 * KD * TOK).rearrange("p (m t) -> p m t", m=2 * KD)
        h2T = part(at8 + 4096, KD * TOK).rearrange("p (k t) -> p k t", k=KD)
        shift = part(at8 + 8192, D)
        scale = part(at8 + 9216, D)
        gain1 = part(at8 + 10240, D)
        yaT = part(at8 + 11264, KA * TOK).rearrange("p (m t) -> p m t", m=KA)

        squares = part(at8 + 6144, D)
        bm = part(at8 + 4096, D)[0:NMOD, :]
        cb_rows = part(at8 + 5120, P)[0:KD + 2 * KD, :]

        gu_w = [part(b * 4 * PAGE, 4 * PAGE).rearrange("p (k s f) -> p k s f", k=KD, s=2) for b in range(2)]
        dlo_w = [page(8 + b).rearrange("p (k d) -> p k d", k=4) for b in range(2)]
        dhi_w = page(10).rearrange("p (k d) -> p k d", k=4)
        x1_back = page(0, TT * D).rearrange("p (t d) -> p t d", t=TT)
        y_out = page(1, TT * D).rearrange("p (t d) -> p t d", t=TT)

        h_sb = sb("h_sb", [P, TT, D])
        gain2 = sb("gain2", [P, D])
        ident = sb("ident", [P, P])
        ones = sb("ones", [P, P])
        iota = sb("iota", [P, TOK])
        rank = sb("rank", [P, TT, NEXP])
        gate_tab = sb("gate_tab", [P, TT, NEXP])
        nblk_i = sb("nblk_i", [P, NEXP], I32)
        wide_i = sb("wide_i", [P, NEXP], I32)
        bgu = sb("bgu", [32 + NBR, 2, BR])
        pick = sb("pick", [32 + NBR, NBR, TB])
        work = sb("work", [P, 3200])
        prob = work[:, 0:2 * BW].rearrange("p (b k) -> p b k", b=2)
        probT = work[:, 768:768 + BW]
        ln_g = work[:, 1152:1152 + AW]
        ln_b = work[:, 1664:1664 + AW]
        wr = work[:, 2176:2176 + KD * NEXP].rearrange("p (k e) -> p k e", k=KD)
        before = work[:, 2432:2432 + P]
        brow = work[0:HEADS, 0:BW]
        sel = work[:, 0:128].rearrange("p (t j) -> p t j", t=TT)
        selg = work[:, 128:384].rearrange("p (t c j) -> p t c j", t=TT, c=2)
        hgT = work[:, 384:896]
        actT = work[:, 384:896]
        selgT = work[:, 896:1152].rearrange("p (t n) -> p t n", t=TT)
        y_sb = work[:, 1152:1664]
        hg = work[:, 1664:2176]
        glu = work[:, 1664:2176].rearrange("p (h n) -> p h n", h=2)
        lin = work[:, 2176:2688].rearrange("p (h n) -> p h n", h=2)
        sig = work[:, 2688:3200].rearrange("p (h n) -> p h n", h=2)
        chosen = work[:, 0:64].rearrange("p (t e) -> p t e", t=TT)
        expo = work[:, 64:128].rearrange("p (t e) -> p t e", t=TT)
        over = work[:, 128:384].rearrange("p (e m) -> p e m", m=8)
        nblk_f = work[:, 384:448].rearrange("p (w e) -> p w e", w=2)
        upto = work[:, 448:512].rearrange("p (t e) -> p t e", t=TT)
        small = sb("small", [P, 352])
        c_act = small[:, 0:8]
        c_sig = small[:, 8:16]
        cb_col = small[:, 16:40]
        c_col = small[:, 16:24]
        bg_col = small[:, 24:40]
        ssq = small[:, 40:52]
        rms = small[:, 52:60]
        rstd = small[:, 60:68]
        part_ms = small[:, 68:72]
        stats = small[:, 72:84].rearrange("p (t s) -> p t s", t=TT)
        meanvar = small[:, 84:88].rearrange("p (t s) -> p t s", t=TT)
        nmax = small[:, 88:92].rearrange("p (b s) -> p b s", b=2)
        psm = small[:, 92:96].rearrange("p (b s) -> p b s", b=2)
        prc = small[:, 96:100].rearrange("p (b s) -> p b s", b=2)
        eps_col = small[:, 100:101]
        b_rt = small[:, 104:136]
        logit = small[:, 136:200].rearrange("p (t e) -> p t e", t=TT)
        top8 = small[:, 200:216].rearrange("p (t e) -> p t e", t=TT)
        above = small[:, 216:280].rearrange("p (t e) -> p t e", t=TT)
        equal = small[:, 280:344].rearrange("p (t e) -> p t e", t=TT)
        r1 = small[:, 344:352]

        UP, TOKS, TURN = (0, 1), 2, 3
        pp = psum("pp", [P, 4, 512])
        po = psum("po", [P, 4, 512])

        bias_rows = nc.dram_tensor("bias_rows", [HEADS, P, BW], F32)
        x1_dram = nc.dram_tensor("x1_dram", [P, TT, D], F32)

        s_page = [sem(f"s_page{i}") for i in range(RING)]
        s_dve_page = sem("s_dve_page")
        s_x, s_c, s_ws, s_bm = sem("s_x"), sem("s_c"), sem("s_ws"), sem("s_bm")
        s_ln, s_bs, s_wr = sem("s_ln"), sem("s_bs"), sem("s_wr")
        s_brow, s_bfill, s_brows, s_bias, s_bmask = (sem("s_brow"), sem("s_bfill"), sem("s_brows"),
                                                     sem("s_bias"), sem("s_bmask"))
        s_gain = [sem(f"s_gain{i}") for i in range(4)]
        s_const, s_pool = sem("s_const"), sem("s_pool")
        s_cT, s_csig, s_cact = sem("s_cT"), sem("s_csig"), sem("s_cact")
        s_adasum, s_mod_a, s_mod_v = sem("s_adasum"), sem("s_mod_a"), sem("s_mod_v")
        s_wsm = sem("s_wsm")
        s_ssx, s_scale, s_h = sem("s_ssx"), sem("s_scale"), sem("s_h")
        s_proj, s_projev = sem("s_proj"), sem("s_projev")
        s_mv, s_lnsq, s_lnn, s_lng, s_lnd = sem("s_mv"), sem("s_lnsq"), sem("s_lnn"), sem("s_lng"), sem("s_lnd")
        s_sgu, s_yb = sem("s_sgu"), sem("s_yb")
        s_score, s_soft, s_exp, s_prob = sem("s_score"), sem("s_soft"), sem("s_exp"), sem("s_prob")
        s_pT, s_pTev, s_pv, s_ya = sem("s_pT"), sem("s_pTev"), sem("s_pv"), sem("s_ya")
        s_br, s_mg, s_merged = sem("s_br"), sem("s_mg"), sem("s_merged")
        s_wo, s_sqh, s_ug, s_ssy = sem("s_wo"), sem("s_sqh"), sem("s_ug"), sem("s_ssy")
        s_x1, s_ssx1, s_h2 = sem("s_x1"), sem("s_ssx1"), sem("s_h2")
        s_spill, s_h2p, s_h2T, s_lg, s_ngm, s_ex = (sem("s_spill"), sem("s_h2p"), sem("s_h2T"), sem("s_lg"),
                                                    sem("s_ngm"), sem("s_ex"))
        s_chosen, s_rank, s_tabs, s_gT = sem("s_chosen"), sem("s_rank"), sem("s_tabs"), sem("s_gT")
        s_gates, s_bd, s_zero = sem("s_gates"), sem("s_bd"), sem("s_zero")
        s_dve = sem("s_dve")
        s_act = sem("s_act")
        s_gup = [[sem(f"s_gup{b}{i}") for i in range(4)] for b in range(2)]
        s_bgu = [sem(f"s_bgu{b}") for b in range(2)]
        s_dlo = [sem(f"s_dlo{b}") for b in range(2)]
        s_dhi = sem("s_dhi")
        s_sel, s_hg, s_hgs, s_turn, s_turned = sem("s_sel"), sem("s_hg"), sem("s_hgs"), sem("s_turn"), sem("s_turned")
        s_selT, s_selTev = sem("s_selT"), sem("s_selTev")
        s_gu, s_glu, s_lin, s_sig = sem("s_gu"), sem("s_glu"), sem("s_lin"), sem("s_sig")
        s_tmp, s_actv, s_aT, s_aTev = sem("s_tmp"), sem("s_actv"), sem("s_aT"), sem("s_aTev")
        s_y, s_ysb = sem("s_y"), sem("s_ysb")
        s_fin, s_sqf, s_uf, s_ssf = sem("s_fin"), sem("s_sqf"), sem("s_uf"), sem("s_ssf")
        s_x1b, s_yo, s_out = sem("s_x1b"), sem("s_yo"), sem("s_out")

        ada_v = w_ada[0].rearrange("(k p) n -> p k n", p=P)
        in_v = w_in[0].rearrange("(k p) n -> p k n", p=P)
        gate_v = w_gate[0].rearrange("(k p) n -> p k n", p=P)
        ba_v = w_branch_a[0].rearrange("(k p) n -> p k n", p=P)
        bb_v = w_branch_b[0].rearrange("(k p) n -> p k n", p=P)
        wo_v = w_out[0].rearrange("(k p) n -> p k n", p=P)
        gu_v = w_gate_up[0].rearrange("e (k p) n -> e p k n", p=P)
        dn_v = w_down[0].rearrange("e (k p) n -> e p k n", p=P)
        bgu_v = b_gate_up[0].rearrange("e (s r f) -> e r s f", s=2, r=NBR)
        x_v = x[0].rearrange("(t p) d -> p t d", p=P)
        out_v = out[0].rearrange("(t p) d -> p t d", p=P)

        def page_src(n):
            _, name, i, half = PAGES[n]
            if name == "ada":
                return ada_v[:, 4 * half:4 * half + 4, i * D:(i + 1) * D]
            if name == "gate":
                return gate_v[:, :, i * 512:(i + 1) * 512]
            if name == "wo":
                return wo_v[:, 4 * i:4 * i + 4, :]
            if name in ("ba", "bb"):
                return {"ba": ba_v, "bb": bb_v}[name]
            return in_v[:, :, IN_COL[name]:IN_COL[name] + AW]

        def page_k(n, k):
            cols = D if PAGES[n][1] in ("ada", "wo", "ba", "bb") else AW
            return page(n % RING)[:, k * cols:(k + 1) * cols]

        def page_landed(eng, n):
            eng.wait_ge(s_page[n % RING], 16 * (n // RING + 1))

        def page_free(eng, n):
            signal, count = consumed(n)
            eng.wait_ge({"dve_page": s_dve_page, "branch": s_br, "wo": s_wo, "proj": s_proj}[signal], count)

        block = ctx.enter_context(nc.Block())

        @block.sync
        def _(sp):
            def small_loads(n):
                if n == 0:
                    sp.dma_start(cb_rows[0:KD, :], c.rearrange("a (k p) -> (a k) p", p=P)).then_inc(s_c, 16)
                    sp.dma_start(cb_rows[KD:3 * KD, :], b_gate.rearrange("a (k p) -> (a k) p", p=P)).then_inc(s_c, 16)
                    sp.dma_start(bm, b_ada.rearrange("a (n d) -> (a n) d", d=D)).then_inc(s_bm, 16)
                if n == 4:
                    sp.dma_start(x_sb, x_v).then_inc(s_x, 16)
                    sp.dma_start(scale, g_pre_mix[0:1, :].to_broadcast([P, D])).then_inc(s_gain[0], 16)
                if n == 6:
                    sp.dma_start(ws, w_spatial[0].rearrange("g t s -> t g s")).then_inc(s_ws, 16)
                    sp.dma_start(brow[:, P - 1:BW], rel_rev[0]).then_inc(s_brow, 16)
                    sp.dma_start(gain1, g_post_mix[0:1, :].to_broadcast([P, D])).then_inc(s_gain[1], 16)
                if n == 8:
                    sp.dma_start(gain2[:], g_post_ffn[0:1, :].to_broadcast([P, D])).then_inc(s_gain[3], 16)
                    sp.dma_start(ln_g, sgu_ln_g[0:1, :].to_broadcast([P, AW])).then_inc(s_ln, 16)
                    sp.dma_start(ln_b, sgu_ln_b[0:1, :].to_broadcast([P, AW])).then_inc(s_ln, 16)
                    sp.dma_start(wr, w_router[0].rearrange("(k p) e -> p k e", p=P)).then_inc(s_wr, 16)
                    sp.dma_start(b_rt, b_router[0:1, :].to_broadcast([P, NEXP])).then_inc(s_wr, 16)
                    for r in range(2):
                        sp.dma_start(bsb[HD * r:HD * r + HD, :, :],
                                     bs_v[r:r + 1].to_broadcast([HD, KA, P])).then_inc(s_bs, 16)

            bs_v = b_spatial[0].rearrange("(m r) t -> r m t", r=2)
            def load_bgu(slot, e):
                sp.dma_start(bgu[32 * slot:32 * slot + NBR, :, :], bgu_v[e]).then_inc(s_bgu[slot], 16)

            def load_gu(slot, e, i):
                sp.dma_start(gu_w[slot][:, 2 * i:2 * i + 2, :, :].rearrange("p k s f -> p k (s f)"),
                             gu_v[e, :, 2 * i:2 * i + 2, :]).then_inc(s_gup[slot][i], 16)

            for n in range(len(PAGES)):
                small_loads(n)
                if n == page_of("gate", 3):
                    sp.wait_ge(s_sgu, KA // 2)
                    load_gu(1, 1, 1)
                if n == page_of("wo", 0):
                    sp.wait_ge(s_zero, 2)
                    for j in range(2):
                        sp.dma_start(y_sb[j * TB:j * TB + NEXP, :],
                                     b_down[0][:, j * 512:(j + 1) * 512]).then_inc(s_bd, 16)
                if n >= RING:
                    page_free(sp, n - RING)
                src = page_src(n)
                sp.dma_start(page(n % RING).rearrange("p (k n) -> p k n", k=src.shape[1]),
                             src).then_inc(s_page[n % RING], 16)

            def load_dlo(slot, e):
                sp.dma_start(dlo_w[slot], dn_v[e, :, 0:4, :]).then_inc(s_dlo[slot], 16)

            def load_dhi(e):
                sp.dma_start(dhi_w, dn_v[e, :, 4:8, :]).then_inc(s_dhi, 16)

            load_bgu(0, 0)
            load_bgu(1, 1)
            page_free(sp, page_of("gate", 3))
            load_gu(0, 0, 0)
            sp.wait_ge(s_pv, HEADS)
            load_gu(1, 1, 2)
            page_free(sp, page_of("ba"))
            for slot, i in ((0, 1), (0, 2), (1, 3)):
                load_gu(slot, slot, i)
            page_free(sp, page_of("wo", 1))
            load_gu(0, 0, 3)
            load_gu(1, 1, 0)
            sp.wait_ge(s_spill, 16 * TT)
            sp.wait_ge(s_h2, 2 * TT)
            load_dlo(0, 0)
            load_dhi(0)
            sp.wait_ge(s_lg, TT)
            load_dlo(1, 1)
            sp.wait_ge(s_tabs, 1)
            done = sp.alloc_register("sp_blocks")
            sp.reg_mov(done, 0)

            def count_blocks(e):
                nb = sp.value_load(nblk_i[0:1, bass.ds(e, 1)], min_val=1, max_val=NBLK)
                sp.reg_add(done, done, nb)
                return sp.snap(done, min_val=1, max_val=NEXP * NBLK)

            total = count_blocks(0)
            with sp.Fori(0, NEXP // 2 - 1) as i:
                for slot in range(2):
                    e = i * 2 + (2 + slot)
                    total = sp.snap(done, min_val=1, max_val=NEXP * NBLK)
                    sp.wait_ge(s_gu, total * 2)
                    load_bgu(slot, e)
                    load_gu(slot, e, 0)
                    sp.wait_ge(s_y, total)
                    load_dhi(e - 1)
                    for q in range(1, 4):
                        load_gu(slot, e, q)
                    load_dlo(slot, e)
                    count_blocks(i * 2 + (1 + slot))
            sp.wait_ge(s_y, sp.snap(done, min_val=1, max_val=NEXP * NBLK))
            load_dhi(NEXP - 1)
            sp.dma_start(x1_back, x1_dram[:, :, :]).then_inc(s_x1b, 16)
            for t in range(TT):
                for half in range(2):
                    sp.wait_ge(s_yo, 2 * t + half + 1)
                    cols = slice(half * 512, half * 512 + 512)
                    sp.dma_start(out_v[:, t, cols], y_out[:, t, cols]).then_inc(s_out, 16)
            sp.wait_ge(s_out, 32 * TT)

        @block.gpsimd
        def _(pool):
            g = nc.gpsimd
            g.memset(ident[:], 0.0).then_inc(s_pool, 1)
            g.memset(ones[:], 1.0).then_inc(s_pool, 1)
            g.memset(eps_col, EPS).then_inc(s_pool, 1)
            pool.wait_ge(s_pool, 3)
            g.affine_select(out=ident[:], in_=ident[:], compare_op=ALU.not_equal, fill=1.0, base=0,
                            pattern=[[-1, P]], channel_multiplier=1).then_inc(s_const, 1)
            g.affine_select(out=before, in_=ones[:], compare_op=ALU.is_gt, fill=0.0, base=0,
                            pattern=[[1, P]], channel_multiplier=-1).then_inc(s_const, 1)
            g.iota(iota[:], pattern=[[1, TOK]], base=0, channel_multiplier=0,
                   allow_small_or_imprecise_dtypes=True).then_inc(s_const, 1)
            for slot in range(2):
                pool.wait_ge(s_const, 3 + slot)
                rows = slice(32 * slot, 32 * slot + NBR)
                g.tensor_copy(pick[rows, :, :], ident[rows, rows].rearrange("r (i a) -> r i a", a=1).to_broadcast(
                    [NBR, NBR, TB])).then_inc(s_const, 1)
            pool.wait_ge(s_brow, 16)
            g.tensor_copy(brow[:, 0:P - 1], brow[:, P - 1:P].to_broadcast([HEADS, P - 1])).then_inc(s_bfill, 1)
            pool.wait_ge(s_bfill, 1)
            pool.dma_start(bias_rows[:, :, :],
                           brow.rearrange("h (a m) -> h a m", a=1).to_broadcast([HEADS, P, BW])).then_inc(s_brows, 16)
            pool.wait_ge(s_h, TT)
            pool.dma_start(scale, g_pre_ffn[0:1, :].to_broadcast([P, D])).then_inc(s_gain[2], 16)
            pool.wait_ge(s_brows, 16)
            window = bass.AP(bias_rows, P - 1, [[BW - 1, P], [P * BW, HEADS], [1, TOK]])
            pool.dma_start(bias, window).then_inc(s_bias, 16)
            pool.wait_ge(s_projev, 8)
            g.affine_select(out=wsT, in_=wsT, compare_op=ALU.is_ge, fill=0.0, base=0,
                            pattern=[[0, GROUPS], [1, P]], channel_multiplier=-1).then_inc(s_wsm, 1)
            pool.wait_ge(s_bias, 16)
            g.memset(bias[0:HD, :, TOK - HD:TOK], NEG).then_inc(s_bmask, 1)
            for t in range(TT):
                pool.wait_ge(s_lnn, t + 1)
                pool.wait_ge(s_ln, 32)
                g.tensor_tensor(vv[:, t, :], vv[:, t, :], ln_g, ALU.mult).then_inc(s_lng, 1)
                pool.wait_ge(s_lng, t + 1)
                g.tensor_tensor(vv[:, t, :], vv[:, t, :], ln_b, ALU.add).then_inc(s_lnd, 1)
            for m in range(KD):
                pool.wait_ge(s_mg, m + 1)
                g.tensor_tensor(mergedT[:, m, :], gates[:, m, :], gates[:, KD + m, :],
                                ALU.add).then_inc(s_merged, 1)
            for t in range(TT):
                pool.wait_ge(s_x1, t + 1)
                pool.dma_start(x1_dram[:, t, :], x_sb[:, t, :]).then_inc(s_spill, 16)
            pool.wait_ge(s_spill, 16 * TT)

        @block.scalar
        def _(act):
            a = nc.scalar
            act.wait_ge(s_cact, 1)
            a.activation(c_sig, c_col, ACT.Sigmoid).then_inc(s_csig, 1)
            act.wait_ge(s_x, 16)
            for t in range(TT):
                a.activation(squares, x_sb[:, t, :], ACT.Square, accum_out=ssq[:, t:t + 1]).then_inc(s_act, 1)
                act.wait_ge(s_act, t + 1)
            act.wait_ge(s_pool, 3)
            a.activation(rms[:, 0:2], ssq[:, 0:2], ACT.Sqrt, scale=1.0 / D, bias=eps_col).then_inc(s_ssx, 1)
            act.wait_ge(s_adasum, 1)
            a.copy(shift, po[:, 2:4, :].rearrange("p b n -> p (b n)")).then_inc(s_mod_a, 1)

            bank = 0

            def evac(dst, func, n_banks=1, **kw):
                nonlocal bank
                act.wait_ge(s_proj, bank + 1)
                a.activation(dst, pp[:, bank % 4, :], func, **kw).then_inc(s_projev, 1)
                bank += 1

            def heads(buf, b):
                return buf[:, 2 * b:2 * b + 2, :].rearrange("p m t -> p (m t)")

            for t in range(TT):
                for q in range(2):
                    act.wait_ge(s_proj, bank + 1)
                    a.copy(hT[:, 4 * q:4 * q + 4, t * P:(t + 1) * P],
                           pp[:, bank % 4, :].rearrange("p (k t) -> p k t", k=4)).then_inc(s_projev, 1)
                    bank += 1
            for b in range(2):
                evac(heads(qT, b), ACT.Copy, scale=float(HD) ** -0.5)
            for b in range(2):
                evac(wsT[:, 4 * b:4 * b + 4, :].rearrange("p g t -> p (g t)"), ACT.Copy)
            for b in range(2):
                evac(heads(kT, b), ACT.Copy)
            for t in range(TT):
                evac(v_sb[:, t, :], ACT.Copy)
            act.wait_ge(s_adasum, 4)
            act.wait_ge(s_h, TT)
            a.copy(shift, po[:, 0:2, :].rearrange("p b n -> p (b n)")).then_inc(s_mod_a, 1)
            for t in range(TT):
                evac(vv[:, t, :], ACT.Gelu)
            for b in range(2):
                evac(heads(ybT, b), ACT.Gelu)
            act.wait_ge(s_mv, TT)
            a.activation(rms[:, 2:4], meanvar[:, :, 1], ACT.Sqrt, bias=eps_col).then_inc(s_lnsq, 1)

            def softmax_exp(h):
                act.wait_ge(s_soft, h + 1)
                a.activation(prob[:, h % 2, 0:P], prob[:, h % 2, 0:P], ACT.Exp, bias=nmax[:, h % 2, 0:1],
                             accum_out=psm[:, h % 2, 0:1])
                a.activation(prob[:, h % 2, P:BW], prob[:, h % 2, P:BW], ACT.Exp, bias=nmax[:, h % 2, 1:2],
                             accum_out=psm[:, h % 2, 1:2]).then_inc(s_exp, 1)

            softmax_exp(0)
            for h in range(HEADS):
                for i in range(2):
                    m = 2 * h + i
                    if i == 0:
                        act.wait_ge(s_proj, bank + 1)
                    ins = a.activation(gates[:, m, :], pp[:, bank % 4, i * TOK:(i + 1) * TOK], ACT.Sigmoid,
                                       bias=bg_col[:, m:m + 1])
                ins.then_inc(s_projev, 1)
                bank += 1
                act.wait_ge(s_pT, h + 1)
                a.copy(probT, po[:, 2, 0:BW]).then_inc(s_pTev, 1)
                if h + 1 < HEADS:
                    softmax_exp(h + 1)

            a.preload_act_table(ACT.Sqrt)
            for t in range(TT):
                act.wait_ge(s_wo, t + 1)
                a.activation(squares[:, 0:512], po[:, 2 * t, :], ACT.Square,
                             accum_out=ssq[:, 2 + 2 * t:3 + 2 * t]).then_inc(s_sqh, 1)
                act.wait_ge(s_ug, 2 * t + 1)
                act.wait_ge(s_sqh, 2 * t + 1)
                a.activation(squares[:, 512:D], po[:, 2 * t + 1, :], ACT.Square,
                             accum_out=ssq[:, 3 + 2 * t:4 + 2 * t]).then_inc(s_sqh, 1)
                a.activation(part_ms[:, t:t + 1], ssq[:, 2 + 2 * t:3 + 2 * t], ACT.Identity, scale=1.0 / D,
                             bias=eps_col).then_inc(s_act, 1)
                act.wait_ge(s_sqh, 2 * t + 2)
                act.wait_ge(s_act, TT + 2 * t + 1)
                a.activation(rms[:, 4 + t:5 + t], ssq[:, 3 + 2 * t:4 + 2 * t], ACT.Sqrt, scale=1.0 / D,
                             bias=part_ms[:, t:t + 1]).then_inc(s_ssy, 1)
                act.wait_ge(s_x1, t + 1)
                a.activation(squares, x_sb[:, t, :], ACT.Square, accum_out=ssq[:, 6 + t:7 + t]).then_inc(s_act, 1)
                act.wait_ge(s_act, TT + 2 * t + 2)
                a.activation(rms[:, 6 + t:7 + t], ssq[:, 6 + t:7 + t], ACT.Sqrt, scale=1.0 / D,
                             bias=eps_col).then_inc(s_ssx1, 1)
                if t == TT - 1:
                    a.preload_act_table(ACT.Exp)
                for q in range(2):
                    act.wait_ge(s_h2p, 2 * t + q + 1)
                    a.copy(h2T[:, 4 * q:4 * q + 4, t * P:(t + 1) * P],
                           pp[:, q, :].rearrange("p (k t) -> p k t", k=4)).then_inc(s_h2T, 1)
            act.wait_ge(s_ngm, 1)
            for t in range(TT):
                ins = a.activation(expo[:, t, :], logit[:, t, :], ACT.Exp, bias=r1[:, t:t + 1])
            ins.then_inc(s_ex, 1)
            act.wait_ge(s_gT, 1)
            for j in range(2):
                a.copy(selgT[j * TB:j * TB + NEXP, :, :].rearrange("p t n -> p (t n)"),
                       pp[0:NEXP, TURN, 0:TOK]).then_inc(s_ysb, 1)
            a.preload_act_table(ACT.Sigmoid)

            item = act.alloc_register("act_item")
            act.reg_mov(item, 0)
            first_half = act.alloc_register("act_first_half")
            act.reg_mov(first_half, 1)
            act.wait_ge(s_tabs, 1)
            with act.Fori(0, NEXP) as e:
                nb = act.value_load(nblk_i[0:1, bass.ds(e, 1)], min_val=1, max_val=NBLK)
                wide = act.value_load(wide_i[0:1, bass.ds(e, 1)], min_val=0, max_val=NBLK)

                def block_of(m, it, halves):
                    w = D * m // P
                    act.wait_ge(s_turn, it)
                    a.copy(hgT[:, 0:w], pp[:, TURN, 0:w]).then_inc(s_turned, 1)
                    act.wait_ge(s_selT, it + 1)
                    a.copy(selgT.rearrange("p t n -> p (t n)"), pp[:, TOKS, 0:TT * P]).then_inc(s_selTev, 1)
                    for hh in range(2):
                        act.wait_ge(s_glu, halves[hh])
                        a.activation(sig[:, hh, 0:w // 2], glu[:, hh, 0:w // 2], ACT.Sigmoid,
                                     scale=ALPHA).then_inc(s_sig, 1)
                    for hh in range(2):
                        act.wait_ge(s_aT, halves[hh])
                        a.copy(actT[:, hh * w // 2:(hh + 1) * w // 2],
                               pp[:, (TOKS, TURN)[hh], 0:w // 2]).then_inc(s_aTev, 1)
                    act.wait_ge(s_y, it)
                    if m == TB:
                        a.copy(y_sb, pp[:, UP[0], :]).then_inc(s_ysb, 1)
                        return
                    a.copy(y_sb[:, 0:w], pp[:, UP[0], 0:w])
                    a.copy(y_sb[0:m, w:2 * w], pp[m:2 * m, UP[0], 0:w])
                    a.copy(y_sb[2 * m:3 * m, w:2 * w], pp[3 * m:P, UP[0], 0:w]).then_inc(s_ysb, 1)

                with act.Fori(0, nb) as b:
                    act.reg_add(item, item, 1)
                    it = act.snap(item, min_val=1, max_val=NEXP * NBLK)
                    halves = (act.snap(first_half, min_val=1, max_val=2 * NEXP * NBLK), it * 2)
                    with act.If(b < wide):
                        block_of(TB, it, halves)
                    with act.Else():
                        block_of(NARROW, it, halves)
                    act.reg_add(first_half, first_half, 2)

            a.preload_act_table(ACT.Sqrt)
            for t in range(TT):
                act.wait_ge(s_fin, t + 1)
                a.activation(h_sb[:, t, 0:512], po[:, 2 * t, :], ACT.Square,
                             accum_out=ssq[:, 8 + 2 * t:9 + 2 * t]).then_inc(s_sqf, 1)
                act.wait_ge(s_uf, 2 * t + 1)
                a.activation(h_sb[:, t, 512:D], po[:, 2 * t + 1, :], ACT.Square,
                             accum_out=ssq[:, 9 + 2 * t:10 + 2 * t]).then_inc(s_sqf, 1)
                act.wait_ge(s_sqf, 2 * t + 1)
                a.activation(part_ms[:, 2 + t:3 + t], ssq[:, 8 + 2 * t:9 + 2 * t], ACT.Identity, scale=1.0 / D,
                             bias=eps_col).then_inc(s_act, 1)
                act.wait_ge(s_sqf, 2 * t + 2)
                act.wait_ge(s_act, 3 * TT + t + 1)
                a.activation(rms[:, t:t + 1], ssq[:, 9 + 2 * t:10 + 2 * t], ACT.Sqrt, scale=1.0 / D,
                             bias=part_ms[:, 2 + t:3 + t]).then_inc(s_ssf, 1)

        @block.vector
        def _(dve):
            v = nc.vector
            chain = 0

            def link(ins):
                nonlocal chain
                chain += 1
                ins.then_inc(s_dve, 1)
                dve.wait_ge(s_dve, chain)

            dve.wait_ge(s_cT, 1)
            v.tensor_copy(cb_col, pp[:, 0, 0:3 * KD]).then_inc(s_cact, 1)
            dve.wait_ge(s_csig, 1)
            v.tensor_tensor(c_act, c_col, c_sig, ALU.mult).then_inc(s_cact, 1)
            dve.wait_ge(s_cact, 2)
            dve.wait_ge(s_bm, 16)

            def modulation(n):
                if n >= 2:
                    dve.wait_ge(s_adasum, n - 1)
                for half in range(2):
                    pg = page_of("ada", n, half)
                    page_landed(dve, pg)
                    for k in range(4):
                        kk = 4 * half + k
                        if kk == 0:
                            link(v.tensor_scalar(acc[:, n % 2, :], page_k(pg, k), c_act[:, kk:kk + 1], None, ALU.mult))
                            link(v.scalar_tensor_tensor(out=acc[0:NMOD, n % 2, :], in0=bm, scalar=ident[0:NMOD, n:n + 1],
                                                        in1=acc[0:NMOD, n % 2, :], op0=ALU.mult, op1=ALU.add))
                            continue
                        ins = v.scalar_tensor_tensor(out=acc[:, n % 2, :], in0=page_k(pg, k), scalar=c_act[:, kk:kk + 1],
                                                     in1=acc[:, n % 2, :], op0=ALU.mult, op1=ALU.add)
                        if k < 3:
                            link(ins)
                        else:
                            ins.then_inc(s_dve_page, 1)
                            dve.wait_ge(s_dve_page, 2 * n + half + 1)

            def mod_bank(n):
                return po[:, 2:4, :] if n % 2 == 0 else po[:, 0:2, :]

            def flat2(ap):
                return ap.rearrange("p b n -> p (b n)")

            modulation(0)
            modulation(1)
            dve.wait_ge(s_ssx, 1)
            link(v.reciprocal(rstd[:, 0:2], rms[:, 0:2]))
            dve.wait_ge(s_adasum, 2)
            dve.wait_ge(s_gain[0], 16)
            v.scalar_tensor_tensor(out=scale, in0=flat2(mod_bank(1)), scalar=1.0, in1=scale,
                                   op0=ALU.add, op1=ALU.mult).then_inc(s_scale, 1)
            dve.wait_ge(s_scale, 1)
            dve.wait_ge(s_mod_a, 1)
            for t in range(TT):
                link(v.scalar_tensor_tensor(out=h_sb[:, t, :], in0=x_sb[:, t, :], scalar=rstd[:, t:t + 1], in1=scale,
                                            op0=ALU.mult, op1=ALU.mult))
                v.tensor_tensor(h_sb[:, t, :], h_sb[:, t, :], shift, ALU.add).then_inc(s_h, 1)
            modulation(2)
            dve.wait_ge(s_adasum, 3)
            dve.wait_ge(s_gain[1], 16)
            v.tensor_tensor(gain1, gain1, flat2(mod_bank(2)), ALU.mult).then_inc(s_mod_v, 1)
            modulation(3)
            modulation(4)
            dve.wait_ge(s_adasum, 5)
            dve.wait_ge(s_gain[2], 16)
            v.scalar_tensor_tensor(out=scale, in0=flat2(mod_bank(4)), scalar=1.0, in1=scale,
                                   op0=ALU.add, op1=ALU.mult).then_inc(s_mod_v, 1)
            modulation(5)
            dve.wait_ge(s_adasum, 6)
            dve.wait_ge(s_gain[3], 16)
            v.tensor_tensor(gain2[:], gain2[:], flat2(mod_bank(5)), ALU.mult).then_inc(s_mod_v, 1)

            dve.wait_ge(s_projev, 14)
            for t in range(TT):
                link(v.bn_stats(stats[:, t, :], vv[:, t, :]))
                v.bn_aggr(meanvar[:, t, :], stats[:, t, :]).then_inc(s_mv, 1)
            dve.wait_ge(s_lnsq, 1)
            link(v.reciprocal(rstd[:, 2:4], rms[:, 2:4]))
            for t in range(TT):
                v.tensor_scalar(vv[:, t, :], vv[:, t, :], meanvar[:, t, 0:1], rstd[:, 2 + t:3 + t],
                                ALU.subtract, ALU.mult).then_inc(s_lnn, 1)
            def scores_bias(h):
                dve.wait_ge(s_bmask, 1)
                dve.wait_ge(s_score, h + 1)
                if h >= 2:
                    dve.wait_ge(s_pT, h - 1)
                v.tensor_tensor(prob[:, h % 2, 0:P], po[:, h % 2, 0:P], bias[:, h, P:TOK], ALU.add)
                link(v.tensor_tensor(prob[:, h % 2, P:BW], po[:, h % 2, P:BW], bias[:, h, :], ALU.add))
                v.tensor_reduce(nmax[:, h % 2, 0:1], prob[:, h % 2, 0:P], AX.X, ALU.max, negate=True)
                v.tensor_reduce(nmax[:, h % 2, 1:2], prob[:, h % 2, P:BW], AX.X, ALU.max,
                                negate=True).then_inc(s_soft, 1)

            def normalise(h):
                dve.wait_ge(s_exp, h + 1)
                link(v.reciprocal(prc[:, h % 2, :], psm[:, h % 2, :]))
                v.tensor_scalar(prob[:, h % 2, 0:P], prob[:, h % 2, 0:P], prc[:, h % 2, 0:1], None, ALU.mult)
                v.tensor_scalar(prob[:, h % 2, P:BW], prob[:, h % 2, P:BW], prc[:, h % 2, 1:2], None,
                                ALU.mult).then_inc(s_prob, 1)

            def heads_out(m):
                dve.wait_ge(s_pv, 2 * m + 2)
                v.tensor_copy(yaT[:, m, :], po[:, 3, 0:TOK]).then_inc(s_ya, 1)

            scores_bias(0)
            dve.wait_ge(s_bs, 32)
            dve.wait_ge(s_projev, 16)
            for m in range(KA):
                dve.wait_ge(s_sgu, m // 2 + 1)
                src = po[:, 2 + m // 2, (m % 2) * TOK:(m % 2 + 1) * TOK].rearrange("p (b t) -> p b t", b=TT)
                dst = prob[:, 1, 0:TOK]
                link(v.tensor_tensor(dst.rearrange("p (b t) -> p b t", b=TT), src,
                                     bsb[:, m:m + 1, :].to_broadcast([P, TT, P]), ALU.add))
                v.tensor_tensor(ybT[:, m, :], ybT[:, m, :], dst, ALU.mult).then_inc(s_yb, 1)
                dve.wait_ge(s_yb, m + 1)
            for h in range(HEADS):
                if h + 1 < HEADS:
                    scores_bias(h + 1)
                normalise(h)
                if h >= 2 and h % 2 == 0:
                    heads_out(h // 2 - 1)
            heads_out(KA - 1)
            v.memset(y_sb, 0.0).then_inc(s_zero, 1)
            v.memset(selgT, 0.0).then_inc(s_zero, 1)

            for m in range(KD):
                dve.wait_ge(s_br, m + 1)
                v.tensor_tensor(gates[:, m, :], pp[:, m % 4, 0:TOK], gates[:, m, :], ALU.mult)
                v.tensor_tensor(gates[:, KD + m, :], pp[:, m % 4, TOK:2 * TOK], gates[:, KD + m, :],
                                ALU.mult).then_inc(s_mg, 1)

            dve.wait_ge(s_mod_a, 2)
            for t in range(TT):
                dve.wait_ge(s_wo, t + 1)
                v.tensor_tensor(h_sb[:, t, 512:D], po[:, 2 * t + 1, :], gain1[:, 512:D], ALU.mult).then_inc(s_ug, 1)
                dve.wait_ge(s_sqh, 2 * t + 1)
                v.tensor_tensor(h_sb[:, t, 0:512], po[:, 2 * t, :], gain1[:, 0:512], ALU.mult).then_inc(s_ug, 1)
                dve.wait_ge(s_ug, 2 * t + 2)
                dve.wait_ge(s_ssy, t + 1)
                link(v.reciprocal(rstd[:, 4 + t:5 + t], rms[:, 4 + t:5 + t]))
                v.scalar_tensor_tensor(out=x_sb[:, t, :], in0=h_sb[:, t, :], scalar=rstd[:, 4 + t:5 + t],
                                       in1=x_sb[:, t, :], op0=ALU.mult, op1=ALU.add).then_inc(s_x1, 1)
                dve.wait_ge(s_x1, t + 1)
                link(v.tensor_tensor(h_sb[:, t, :], x_sb[:, t, :], scale, ALU.mult))
                dve.wait_ge(s_ssx1, t + 1)
                link(v.reciprocal(rstd[:, 6 + t:7 + t], rms[:, 6 + t:7 + t]))
                for q in range(2):
                    cols = slice(q * 512, (q + 1) * 512)
                    v.scalar_tensor_tensor(out=h_sb[:, t, cols], in0=h_sb[:, t, cols], scalar=rstd[:, 6 + t:7 + t],
                                           in1=shift[:, cols], op0=ALU.mult, op1=ALU.add).then_inc(s_h2, 1)

            dve.wait_ge(s_wr, 32)
            for t in range(TT):
                dve.wait_ge(s_lg, t + 1)
                link(v.tensor_tensor(logit[:, t, :], pp[:, 2 + t, 0:NEXP], b_rt, ALU.add))
                link(v.max(top8[:, t, :], logit[:, t, :]))
            v.tensor_scalar(r1[:, 0:2], top8[:, :, 0], -1.0, None, ALU.mult).then_inc(s_ngm, 1)
            for t in range(TT):
                fourth = top8[:, t, TOPK - 1:TOPK]
                v.tensor_scalar(above[:, t, :], logit[:, t, :], fourth, None, ALU.is_gt)
                link(v.tensor_scalar(equal[:, t, :], logit[:, t, :], fourth, None, ALU.is_equal))
            link(v.tensor_reduce(r1[:, 2:4], above, AX.X, ALU.add))
            link(v.tensor_scalar(r1[:, 2:4], r1[:, 2:4], -1.0, float(TOPK), ALU.mult, ALU.add))
            for t in range(TT):
                link(v.tensor_tensor_scan(upto[:, t, :], ones[:, 0:NEXP], equal[:, t, :], 0.0, ALU.mult, ALU.add))
                link(v.scalar_tensor_tensor(out=equal[:, t, :], in0=upto[:, t, :], scalar=r1[:, 2 + t:3 + t],
                                            in1=equal[:, t, :], op0=ALU.is_le, op1=ALU.mult))
            v.tensor_tensor(chosen, above, equal, ALU.add).then_inc(s_chosen, 1)
            dve.wait_ge(s_chosen, 1)
            dve.wait_ge(s_ex, 1)
            link(v.tensor_tensor(expo, expo, chosen, ALU.mult))
            link(v.tensor_reduce(r1[:, 4:6], expo, AX.X, ALU.add))
            link(v.reciprocal(r1[:, 6:8], r1[:, 4:6]))
            for t in range(TT):
                ins = v.tensor_scalar(gate_tab[:, t, :], expo[:, t, :], r1[:, 6 + t:7 + t], None, ALU.mult)
            ins.then_inc(s_gates, 1)
            dve.wait_ge(s_gates, 1)
            dve.wait_ge(s_rank, 1)
            dve.wait_ge(s_const, 5)
            counts = pp[:, 0, 2 * NEXP:3 * NEXP].rearrange("p (e a) -> p e a", a=1).to_broadcast([P, NEXP, 8])
            steps = iota[:].rearrange("p (a m n) -> p a m n", a=1, n=NARROW)[:, :, :, NARROW - 1]
            link(v.scalar_tensor_tensor(out=over, in0=counts, scalar=-1.0, in1=steps.to_broadcast([P, NEXP, 8]),
                                        op0=ALU.add, op1=ALU.is_gt))
            for w in range(2):
                ins = v.tensor_reduce(nblk_f[:, w, :], over.rearrange("p e (m w) -> p e m w", w=2)[:, :, :, 1 - w],
                                      AX.X, ALU.add)
            link(ins)
            v.tensor_scalar(nblk_i[:], nblk_f[:, 0, :], 1.0, None, ALU.add)
            v.tensor_copy(wide_i[:], nblk_f[:, 1, :])
            link(v.scalar_tensor_tensor(out=rank[:], in0=pp[:, 0, 0:2 * NEXP].rearrange("p (t e) -> p t e", t=TT),
                                        scalar=1.0, in1=chosen, op0=ALU.add, op1=ALU.mult))
            v.tensor_scalar(rank[:], rank[:], -1.0, None, ALU.add).then_inc(s_tabs, 1)
            dve.wait_ge(s_tabs, 1)

            item = dve.alloc_register("dve_item")
            dve.reg_mov(item, 0)
            first_half = dve.alloc_register("dve_first_half")
            dve.reg_mov(first_half, 1)
            with dve.Fori(0, NEXP) as e:
                nb = dve.value_load(nblk_i[0:1, bass.ds(e, 1)], min_val=1, max_val=NBLK)
                wide = dve.value_load(wide_i[0:1, bass.ds(e, 1)], min_val=0, max_val=NBLK)

                def block_of(m, it, halves):
                    w = D * m // P
                    dve.wait_ge(s_hg, it)
                    v.tensor_copy(hg[:, 0:w], pp[:, TOKS, 0:w]).then_inc(s_hgs, 1)
                    for hh in range(2):
                        n = halves[hh]
                        up, x_glu, x_lin, x_sig = (pp[:, UP[hh], 0:w], glu[:, hh, 0:w // 2], lin[:, hh, 0:w // 2],
                                                   sig[:, hh, 0:w // 2])
                        dve.wait_ge(s_gu, n)
                        v.tensor_scalar(x_glu, up[:, 0:w // 2], LIMIT, None, ALU.min).then_inc(s_glu, 1)
                        v.tensor_scalar(x_lin, up[:, w // 2:w], LIMIT, -LIMIT, ALU.min, ALU.max).then_inc(s_lin, 1)
                        dve.wait_ge(s_lin, n)
                        v.scalar_tensor_tensor(out=x_lin, in0=x_lin, scalar=1.0, in1=x_glu, op0=ALU.add,
                                               op1=ALU.mult).then_inc(s_tmp, 1)
                        dve.wait_ge(s_tmp, n)
                        dve.wait_ge(s_sig, n)
                        v.tensor_tensor(x_sig, x_lin, x_sig, ALU.mult).then_inc(s_actv, 1)

                with dve.Fori(0, nb) as b:
                    dve.reg_add(item, item, 1)
                    it = dve.snap(item, min_val=1, max_val=NEXP * NBLK)
                    halves = (dve.snap(first_half, min_val=1, max_val=2 * NEXP * NBLK), it * 2)
                    dve.wait_ge(s_selT, it)
                    places = iota[:, bass.ds(b * TB, TB)]
                    for t in range(TT):
                        rk = rank[:, t, bass.ds(e, 1)]
                        gt = gate_tab[:, t, bass.ds(e, 1)]
                        v.tensor_scalar(sel[:, t, :], places, rk, None, ALU.is_equal)
                        for c in range(2):
                            ins = v.tensor_scalar(selg[:, t, c, :], places, rk, gt, ALU.is_equal, ALU.mult)
                    ins.then_inc(s_sel, 1)
                    with dve.If(b < wide):
                        block_of(TB, it, halves)
                    with dve.Else():
                        block_of(NARROW, it, halves)
                    dve.reg_add(first_half, first_half, 2)

            dve.wait_ge(s_x1b, 16)
            for t in range(TT):
                dve.wait_ge(s_fin, t + 1)
                v.tensor_tensor(y_out[:, t, 512:D], po[:, 2 * t + 1, :], gain2[:, 512:D], ALU.mult).then_inc(s_uf, 1)
                dve.wait_ge(s_sqf, 2 * t + 1)
                v.tensor_tensor(y_out[:, t, 0:512], po[:, 2 * t, :], gain2[:, 0:512], ALU.mult).then_inc(s_uf, 1)
            for t in range(TT):
                dve.wait_ge(s_uf, 2 * t + 2)
                dve.wait_ge(s_ssf, t + 1)
                link(v.reciprocal(rstd[:, t:t + 1], rms[:, t:t + 1]))
                for half in range(2):
                    cols = slice(half * 512, half * 512 + 512)
                    v.scalar_tensor_tensor(out=y_out[:, t, cols], in0=y_out[:, t, cols], scalar=rstd[:, t:t + 1],
                                           in1=x1_back[:, t, cols], op0=ALU.mult, op1=ALU.add).then_inc(s_yo, 1)

        @block.tensor
        def _(pe):
            t_ = nc.tensor
            pe.wait_ge(s_const, 1)
            pe.wait_ge(s_c, 32)
            t_.transpose(pp[:, 0, 0:3 * KD], cb_rows, ident[0:3 * KD, 0:3 * KD]).then_inc(s_cT, 1)

            def modulation_sum(n):
                if n == 0:
                    pe.wait_ge(s_pool, 2)
                elif n == 2:
                    pe.wait_ge(s_mod_a, 1)
                elif n == 3:
                    pe.wait_ge(s_scale, 1)
                elif n == 4:
                    pe.wait_ge(s_mod_v, 1)
                elif n == 5:
                    pe.wait_ge(s_mod_a, 2)
                pe.wait_ge(s_dve_page, 2 * n + 2)
                for half in range(2):
                    mm = t_.matmul(po[:, 2 * (1 - n % 2) + half, :], ones[:], acc[:, n % 2, half * 512:(half + 1) * 512],
                                   start=True, stop=True)
                mm.then_inc(s_adasum, 1)

            modulation_sum(0)
            modulation_sum(1)

            bank = 0

            def next_bank():
                nonlocal bank
                if bank >= 4:
                    pe.wait_ge(s_projev, bank - 3)
                bank += 1
                return pp[:, (bank - 1) % 4, :]

            for t in range(TT):
                pe.wait_ge(s_h, t + 1)
                for q in range(2):
                    ps = next_bank()
                    for i in range(4):
                        mm = t_.transpose(ps[:, i * P:(i + 1) * P], h_sb[:, t, (4 * q + i) * P:(4 * q + i + 1) * P],
                                          ident[:])
                    mm.then_inc(s_proj, 1)
            pe.wait_ge(s_projev, 4)

            def page_T(name):
                pg = page_of(name)
                page_landed(pe, pg)
                for b in range(2):
                    ps = next_bank()
                    for i in range(2):
                        m = 2 * b + i
                        for k in range(KD):
                            mm = t_.matmul(ps[:, i * TOK:(i + 1) * TOK], page_k(pg, k)[:, m * P:(m + 1) * P],
                                           hT[:, k, :], start=(k == 0), stop=(k == KD - 1))
                    mm.then_inc(s_proj, 1)

            def page_rows(name):
                pg = page_of(name)
                page_landed(pe, pg)
                for t in range(TT):
                    ps = next_bank()
                    for k in range(KD):
                        mm = t_.matmul(ps, hT[:, k, t * P:(t + 1) * P], page_k(pg, k), start=(k == 0),
                                       stop=(k == KD - 1))
                    mm.then_inc(s_proj, 1)

            page_T("q")
            pe.wait_ge(s_ws, 16)
            for b in range(2):
                ps = next_bank()
                for i in range(4):
                    mm = t_.transpose(ps[:, i * P:(i + 1) * P], ws[:, 4 * b + i, :], ident[:])
                mm.then_inc(s_proj, 1)
            modulation_sum(2)
            page_T("k")
            page_rows("v")
            modulation_sum(3)
            page_rows("vv")
            modulation_sum(4)
            page_T("u")
            modulation_sum(5)

            def spatial():
                pe.wait_ge(s_lnd, TT)
                pe.wait_ge(s_wsm, 1)
                pe.wait_ge(s_mod_v, 2)
                for m in range(KA):
                    for r in range(2):
                        for b in range(TT):
                            g = 2 * m + r
                            col = (m % 2) * TOK + b * P
                            mm = t_.matmul(po[HD * r:HD * r + HD, 2 + m // 2, col:col + P],
                                           vv[:, b, g * HD:(g + 1) * HD], wsT[:, g, :], start=True, stop=True)
                    if m % 2:
                        mm.then_inc(s_sgu, 1)

            def scores(h):
                m, r = h // 2, HD * (h % 2)
                if h == 0:
                    pe.wait_ge(s_projev, 10)
                    pe.wait_ge(s_mod_v, 3)
                if h >= 2:
                    pe.wait_ge(s_soft, h - 1)
                t_.matmul(po[:, h % 2, 0:P], qT[r:r + HD, m, 0:P], kT[r:r + HD, m, 0:P], start=True, stop=True)
                t_.matmul(po[:, h % 2, P:BW], qT[r:r + HD, m, P:TOK], kT[r:r + HD, m, :], start=True,
                          stop=True).then_inc(s_score, 1)

            scores(0)
            scores(1)

            def gate_group(n):
                pg = page_of("gate", n // 2)
                if n % 2 == 0:
                    page_landed(pe, pg)
                ps = next_bank()
                for i in range(2):
                    m = 2 * (n % 2) + i
                    for k in range(KD):
                        mm = t_.matmul(ps[:, i * TOK:(i + 1) * TOK], page_k(pg, k)[:, m * P:(m + 1) * P], hT[:, k, :],
                                       start=(k == 0), stop=(k == KD - 1))
                mm.then_inc(s_proj, 1)

            def branch(m, name, src):
                if m >= 4:
                    pe.wait_ge(s_mg, m - 3)
                else:
                    pe.wait_ge(s_projev, bank - 3 + m)
                page_landed(pe, page_of(name))
                half = ("ba", "bb").index(name)
                for k in range(KA):
                    mm = t_.matmul(pp[:, m % 4, half * TOK:(half + 1) * TOK],
                                   page_k(page_of(name), k)[:, m * P:(m + 1) * P], src[:, k, :], start=(k == 0),
                                   stop=(k == KA - 1))
                return mm

            def values(h):
                pe.wait_ge(s_pTev, h + 1)
                if h >= 2 and h % 2 == 0:
                    pe.wait_ge(s_ya, h // 2)
                r, col = HD * (h % 2), 0
                t_.matmul(po[r:r + HD, 3, col:col + P], v_sb[:, 0, h * HD:(h + 1) * HD], probT[:, 0:P], start=True,
                          stop=True)
                for b in range(TT):
                    mm = t_.matmul(po[r:r + HD, 3, col + P:col + TOK], v_sb[:, b, h * HD:(h + 1) * HD],
                                   probT[:, (1 + b) * P:(2 + b) * P], start=(b == 0), stop=(b == 1))
                mm.then_inc(s_pv, 1)

            gate_group(0)
            spatial()
            for h in range(HEADS):
                if h + 1 < HEADS:
                    gate_group(h + 1)
                else:
                    branch(0, "bb", ybT)
                    branch(1, "bb", ybT)
                if h:
                    values(h - 1)
                pe.wait_ge(s_prob, h + 1)
                if h == 0:
                    pe.wait_ge(s_yb, KA)
                for i in range(3):
                    mm = t_.transpose(po[:, 2, i * P:(i + 1) * P], prob[:, h % 2, i * P:(i + 1) * P], ident[:])
                mm.then_inc(s_pT, 1)
                if h + 2 < HEADS:
                    scores(h + 2)
            branch(2, "bb", ybT)
            values(HEADS - 1)
            branch(3, "bb", ybT)

            pe.wait_ge(s_ya, KA)
            for m in range(KD):
                if m >= 4:
                    branch(m, "bb", ybT)
                branch(m, "ba", yaT).then_inc(s_br, 1)

            for i in range(2):
                page_landed(pe, page_of("wo", i))
            for t in range(TT):
                for k in range(KD):
                    if t == 0:
                        pe.wait_ge(s_merged, k + 1)
                    for half in range(2):
                        mm = t_.matmul(po[:, 2 * t + half, :], mergedT[:, k, t * P:(t + 1) * P],
                                       page_k(page_of("wo", k // 4), k % 4)[:, half * 512:(half + 1) * 512],
                                       start=(k == 0), stop=(k == KD - 1))
                mm.then_inc(s_wo, 1)

            pe.wait_ge(s_wr, 32)
            pe.wait_ge(s_mg, KD)
            for t in range(TT):
                for q in range(2):
                    pe.wait_ge(s_h2, 2 * t + q + 1)
                    if t:
                        pe.wait_ge(s_h2T, q + 1)
                    for i in range(4):
                        mm = t_.transpose(pp[:, q, i * P:(i + 1) * P], h_sb[:, t, (4 * q + i) * P:(4 * q + i + 1) * P],
                                          ident[:])
                    mm.then_inc(s_h2p, 1)
                for k in range(KD):
                    if k % 4 == 0:
                        pe.wait_ge(s_h2T, 2 * t + k // 4 + 1)
                    mm = t_.matmul(pp[:, 2 + t, 0:NEXP], h2T[:, k, t * P:(t + 1) * P], wr[:, k, :], start=(k == 0),
                                   stop=(k == KD - 1))
                mm.then_inc(s_lg, 1)

            zeros = selgT.rearrange("p t n -> p (t n)").bitcast(BF16)
            for b in range(4):
                mm = t_.matmul(po[:, b, :], zeros[:, 0:P], zeros, start=True, stop=False, skip_group_check=True)
            mm.then_inc(s_selT, 1)
            pe.wait_ge(s_const, 5)
            pe.wait_ge(s_chosen, 1)
            t_.matmul(pp[:, 0, 0:NEXP], before, chosen[:, 0, :], start=True, stop=True)
            for col, second in ((NEXP, before), (2 * NEXP, ones[:])):
                t_.matmul(pp[:, 0, col:col + NEXP], ones[:], chosen[:, 0, :], start=True, stop=False)
                mm = t_.matmul(pp[:, 0, col:col + NEXP], second, chosen[:, 1, :], start=False, stop=True)
            mm.then_inc(s_rank, 1)
            pe.wait_ge(s_gates, 1)
            for t in range(TT):
                mm = t_.transpose(pp[0:NEXP, TURN, t * P:(t + 1) * P], gate_tab[:, t, :], ident[:])
            mm.then_inc(s_gT, 1)
            pe.wait_ge(s_bd, 32)
            pe.wait_ge(s_tabs, 1)

            def combine(it, last=False):
                pe.wait_ge(s_ysb, it + 1)
                for t in range(TT):
                    for j in range(2):
                        mm = t_.matmul(po[:, 2 * t + j, :], selgT[j * TB:(j + 1) * TB, t, :],
                                       y_sb[j * TB:(j + 1) * TB, :], start=False, stop=last, skip_group_check=True)
                    if last:
                        mm.then_inc(s_fin, 1)

            def block_of(m, it, halves, slot, landed, dhi_landed):
                tiles, w = P // m, D * m // P
                q = w // P
                pe.wait_ge(s_sel, it)
                for t in range(TT):
                    for j in range(tiles):
                        mm = t_.matmul(pp[j * m:(j + 1) * m, TOKS, 0:w], sel[:, t, 0:m],
                                       h_sb[:, t, j * w:(j + 1) * w], start=(t == 0), stop=(t == TT - 1))
                mm.then_inc(s_hg, 1)
                combine(it)
                pe.wait_ge(s_hgs, it)
                for i in range(q):
                    mm = t_.transpose(pp[:, TURN, i * P:(i + 1) * P], hg[:, i * P:(i + 1) * P], ident[:])
                mm.then_inc(s_turn, 1)
                pe.wait_ge(s_bgu[slot], landed)
                for t in range(TT):
                    mm = t_.transpose(pp[:, TOKS, t * P:(t + 1) * P], selg[:, t, :, :].rearrange("p c j -> p (c j)"),
                                      ident[:])
                mm.then_inc(s_selT, 1)
                rows = slice(32 * slot, 32 * slot + NBR)
                for hh in range(2):
                    for j in range(tiles):
                        r, off = divmod(j * w + hh * w // 2, BR)
                        t_.matmul(pp[j * m:(j + 1) * m, UP[hh], 0:w].rearrange("p (s f) -> p s f", s=2),
                                  pick[rows, r, 0:m], bgu[rows, :, off:off + w // 2], start=True, stop=False,
                                  skip_group_check=True)
                pe.wait_ge(s_turned, it)
                for hh in range(2):
                    for k in range(KD):
                        if hh == 0 and k % 2 == 0:
                            pe.wait_ge(s_gup[slot][k // 2], landed)
                        at = (k % q) * P + (k // q) * m
                        for j in range(tiles):
                            col = j * w + hh * w // 2
                            mm = t_.matmul(pp[j * m:(j + 1) * m, UP[hh], 0:w].rearrange("p (s f) -> p s f", s=2),
                                           hgT[:, at:at + m], gu_w[slot][:, k, :, col:col + w // 2], start=False,
                                           stop=(k == KD - 1), skip_group_check=True)
                    mm.then_inc(s_gu, 1)

                def turn_half(hh):
                    pe.wait_ge(s_actv, halves[hh])
                    for i in range(q // 2):
                        mm = t_.transpose(pp[:, (TOKS, TURN)[hh], i * P:(i + 1) * P], sig[:, hh, i * P:(i + 1) * P],
                                          ident[:])
                    mm.then_inc(s_aT, 1)

                pe.wait_ge(s_selTev, it)
                turn_half(0)
                pe.wait_ge(s_dlo[slot], landed)
                pe.wait_ge(s_aTev, halves[0])
                order = sorted(range(KD), key=lambda k: (k % q >= q // 2, k))
                for n, k in enumerate(order):
                    if k == 4:
                        pe.wait_ge(s_dhi, dhi_landed)
                    if n == KD // 2 - 1:
                        turn_half(1)
                    if n == KD // 2:
                        pe.wait_ge(s_aTev, halves[1])
                    wd = dlo_w[slot][:, k, :] if k < 4 else dhi_w[:, k - 4, :]
                    at = (k % q) * P + (k // q) * m
                    for j in range(tiles):
                        mm = t_.matmul(pp[j * m:(j + 1) * m, UP[0], 0:w], actT[:, at:at + m],
                                       wd[:, j * w:(j + 1) * w], start=(n == 0), stop=(n == KD - 1))
                mm.then_inc(s_y, 1)

            item = pe.alloc_register("pe_item")
            pe.reg_mov(item, 0)
            first_half = pe.alloc_register("pe_first_half")
            pe.reg_mov(first_half, 1)
            with pe.Fori(0, NEXP // 2) as i:
                for slot in range(2):
                    nb = pe.value_load(nblk_i[0:1, bass.ds(i * 2 + slot, 1)], min_val=1, max_val=NBLK)
                    wide = pe.value_load(wide_i[0:1, bass.ds(i * 2 + slot, 1)], min_val=0, max_val=NBLK)
                    with pe.Fori(0, nb) as b:
                        pe.reg_add(item, item, 1)
                        it = pe.snap(item, min_val=1, max_val=NEXP * NBLK)
                        halves = (pe.snap(first_half, min_val=1, max_val=2 * NEXP * NBLK), it * 2)
                        landed, dhi_landed = i * 16 + 16, i * 32 + 16 * (slot + 1)
                        with pe.If(b < wide):
                            block_of(TB, it, halves, slot, landed, dhi_landed)
                        with pe.Else():
                            block_of(NARROW, it, halves, slot, landed, dhi_landed)
                        pe.reg_add(first_half, first_half, 2)
            pe.reg_add(item, item, 1)
            combine(pe.snap(item, min_val=1, max_val=NEXP * NBLK + 1), last=True)


_INS = ["x", "c", "w_ada", "b_ada", "g_pre_mix", "g_post_mix", "w_in", "rel_bias", "sgu_ln_g", "sgu_ln_b",
        "w_spatial", "b_spatial", "w_branch_a", "w_branch_b", "w_gate", "b_gate", "w_out", "g_pre_ffn",
        "g_post_ffn", "w_router", "b_router", "w_gate_up", "b_gate_up", "w_down", "b_down"]
_OUTS = [((1, TOK, D), "float32")]


def kernel(**inputs):
    import numpy as _np
    import concourse.bacc as _bacc
    from concourse import mybir as _mybir
    from concourse.bass_utils import run_bass_kernel_spmd as _run

    nc = _bacc.Bacc("TRN2", target_bir_lowering=False, num_devices=1)
    arrays, args = {}, []
    for name in _INS:
        a = _np.asarray(inputs[name])
        if name == "rel_bias":
            a = a[:, :, ::-1]
        a = _np.ascontiguousarray(a)
        arrays[f"in_{name}_dram"] = a
        args.append(nc.dram_tensor(f"in_{name}_dram", a.shape, _mybir.dt.from_np(a.dtype), kind="ExternalInput").ap())
    for i, (shape, dtype) in enumerate(_OUTS):
        dt = _mybir.dt.from_np(_np.dtype(dtype))
        args.append(nc.dram_tensor(f"out_{i}_dram", shape, dt, kind="ExternalOutput").ap())
    block_program(nc, *args)
    r = _run(nc, [arrays], core_ids=[0])
    return r.results[0]["out_0_dram"]
```
